# Optimizing a Trainium2 kernel written in Bass

```python
import jax, jax.numpy as jnp
from jax import lax
import numpy as np

D_MODEL = 1024
BATCH = 1
SEQ = 2048
DEPTH = 1

CHUNK = 64
N_META = 16
LEAD_PAD = CHUNK - N_META
EPS = 1e-6
MIX_WIDTH = D_MODEL
M_HEADS = 4
M_WIDTH = MIX_WIDTH // 2
M_HEAD_DIM = M_WIDTH // M_HEADS
CONV_K = 4
G_HEADS = 4
G_WIDTH = MIX_WIDTH - M_WIDTH
G_V_DIM = G_WIDTH // G_HEADS
G_K_DIM = G_V_DIM // 2
G_K_WIDTH = G_HEADS * G_K_DIM
G_RANK = 16
G_TAU = 16.0
N_GROUPS = 4
EXPERTS_PER_GROUP = 8
N_EXPERTS = N_GROUPS * EXPERTS_PER_GROUP
TOP_K = 2
D_EXPERT = D_MODEL // 4
EXPERT_BLOCK = 128
IN_SPLITS = (2 * M_WIDTH, M_WIDTH, M_WIDTH, M_HEADS, M_HEADS, G_K_WIDTH, G_K_WIDTH, G_WIDTH, G_WIDTH, G_RANK)
IN_WIDTH = sum(IN_SPLITS)
F32 = jnp.float32

kernel_name = "hybrid_mlstm_gla_hiermoe"

def rmsnorm(x, g):
    xf = x.astype(F32)
    y = xf * lax.rsqrt(jnp.mean(xf * xf, axis=-1, keepdims=True) + EPS)
    return (y * g.astype(F32)).astype(x.dtype)

def head_rmsnorm(h, g):
    y = h * lax.rsqrt(jnp.mean(h * h, axis=-1, keepdims=True) + EPS)
    return y.reshape(h.shape[0], h.shape[1], -1) * g.astype(F32)

def causal_depthwise_conv(x, w, b):
    c = x.shape[-1]
    y = lax.conv_general_dilated(x, w[:, None, :], window_strides=(1,), padding=[(CONV_K - 1, 0)],
                                 dimension_numbers=('NWC', 'WIO', 'NWC'), feature_group_count=c)
    return y + b

def to_chunks(t, fill):
    pad = [(0, 0), (LEAD_PAD, 0)] + [(0, 0)] * (t.ndim - 2)
    t = jnp.pad(t, pad, constant_values=fill)
    bn, lp = t.shape[0], t.shape[1]
    t = t.reshape(bn, lp // CHUNK, CHUNK, *t.shape[2:])
    return jnp.moveaxis(t, (1, 3), (0, 2))

def from_chunks(h):
    h = jnp.moveaxis(h, (0, 2), (1, 3))
    bn, nc, c, nh, d = h.shape
    return h.reshape(bn, nc * c, nh, d)[:, LEAD_PAD:]

def mlstm_heads(q, k, v, ig, lf):
    bn, _, nh, d = q.shape
    causal = jnp.tril(jnp.ones((CHUNK, CHUNK), dtype=bool))
    xs = (to_chunks(q, 0.0), to_chunks(k, 0.0), to_chunks(v, 0.0),
          to_chunks(ig, -jnp.inf), to_chunks(lf, 0.0))

    def step(carry, inp):
        c_state, n_state, m_state = carry
        qc, kc, vc, igc, lfc = inp
        b = jnp.cumsum(lfc, axis=-1)
        dmat = jnp.where(causal, b[..., :, None] - b[..., None, :] + igc[..., None, :], -jnp.inf)
        m_inter = b + m_state[..., None]
        m_t = jnp.maximum(m_inter, jnp.max(dmat, axis=-1))
        s = jnp.einsum('bhtd,bhsd->bhts', qc, kc) * jnp.exp(dmat - m_t[..., None])
        w_inter = jnp.exp(m_inter - m_t)
        num = jnp.einsum('bhts,bhsv->bhtv', s, vc) + w_inter[..., None] * jnp.einsum('bhvk,bhtk->bhtv', c_state, qc)
        den = jnp.sum(s, axis=-1) + w_inter * jnp.einsum('bhk,bhtk->bht', n_state, qc)
        h = num / jnp.maximum(jnp.abs(den), jnp.exp(-m_t))[..., None]
        b_end = b[..., -1]
        g = b_end[..., None] - b + igc
        m_new = jnp.maximum(b_end + m_state, jnp.max(g, axis=-1))
        wk = jnp.exp(g - m_new[..., None])
        decay = jnp.exp(b_end + m_state - m_new)
        c_state = decay[..., None, None] * c_state + jnp.einsum('bhs,bhsv,bhsk->bhvk', wk, vc, kc)
        n_state = decay[..., None] * n_state + jnp.einsum('bhs,bhsk->bhk', wk, kc)
        return (c_state, n_state, m_new), h

    init = (jnp.zeros((bn, nh, d, d), F32), jnp.zeros((bn, nh, d), F32), jnp.zeros((bn, nh), F32))
    _, h = lax.scan(step, init, xs)
    return from_chunks(h)

def gla_heads(q, k, v, la):
    bn, _, nh, dk = q.shape
    dv = v.shape[-1]
    causal = jnp.tril(jnp.ones((CHUNK, CHUNK), dtype=bool))
    xs = (to_chunks(q, 0.0), to_chunks(k, 0.0), to_chunks(v, 0.0), to_chunks(la, 0.0))

    def step(s_state, inp):
        qc, kc, vc, lac = inp
        b = jnp.cumsum(lac, axis=2)
        pair = jnp.where(causal[:, :, None], b[:, :, :, None, :] - b[:, :, None, :, :], -jnp.inf)
        a = jnp.einsum('bhtj,bhsj,bhtsj->bhts', qc, kc, jnp.exp(pair))
        o = jnp.einsum('bhts,bhsv->bhtv', a, vc) + jnp.einsum('bhtj,bhjv->bhtv', qc * jnp.exp(b), s_state)
        b_end = b[:, :, -1]
        s_state = jnp.exp(b_end)[..., None] * s_state + jnp.einsum(
            'bhsj,bhsv->bhjv', kc * jnp.exp(b_end[:, :, None] - b), vc)
        return s_state, o

    _, o = lax.scan(step, jnp.zeros((bn, nh, dk, dv), F32), xs)
    return from_chunks(o)

def hybrid_mixer(xn, w_in, conv_w, conv_b, gate_b, m_norm_g, a_w2, a_b, g_norm_g, w_out):
    bn, seq_len, _ = xn.shape
    z = (xn @ w_in).astype(F32)
    qk_m, v_m, o_m, ig, fg, q_g, k_g, v_g, gate_g, code_g = jnp.split(
        z, np.cumsum(IN_SPLITS)[:-1].tolist(), axis=-1)
    heads = lambda t, d: t.reshape(bn, seq_len, -1, d)
    qk_m = jax.nn.silu(causal_depthwise_conv(qk_m, conv_w.astype(F32), conv_b.astype(F32)))
    q_m, k_m = jnp.split(qk_m, 2, axis=-1)
    h_m = mlstm_heads(heads(q_m, M_HEAD_DIM), heads(k_m, M_HEAD_DIM) * (M_HEAD_DIM ** -0.5),
                      heads(v_m, M_HEAD_DIM), ig + gate_b[0].astype(F32),
                      jax.nn.log_sigmoid(fg + gate_b[1].astype(F32)))
    y_m = head_rmsnorm(h_m, m_norm_g) * jax.nn.sigmoid(o_m)
    la = jax.nn.log_sigmoid(code_g @ a_w2.astype(F32) + a_b.astype(F32)) / G_TAU
    h_g = gla_heads(heads(q_g, G_K_DIM) * (G_K_DIM ** -0.5), heads(k_g, G_K_DIM),
                    heads(v_g, G_V_DIM), heads(la, G_K_DIM))
    y_g = head_rmsnorm(h_g, g_norm_g) * jax.nn.silu(gate_g)
    y = jnp.concatenate([y_m, y_g], axis=-1).astype(xn.dtype)
    return y @ w_out

def hierarchical_moe(xn, wr_g, br_g, wr_e, br_e, w_gate, w_up, w_down):
    bn, seq_len, dm = xn.shape
    xt = xn.reshape(-1, dm)
    n_tok = xt.shape[0]
    p_group = jax.nn.softmax((xt @ wr_g).astype(F32) + br_g.astype(F32), axis=-1)
    g_sel = jnp.argmax(p_group, axis=-1)
    p_sel = jnp.take_along_axis(p_group, g_sel[:, None], axis=-1)
    e_logits = ((xt @ wr_e).astype(F32) + br_e.astype(F32)).reshape(n_tok, N_GROUPS, EXPERTS_PER_GROUP)
    e_logits = jnp.take_along_axis(e_logits, g_sel[:, None, None], axis=1)[:, 0]
    top_v, top_i = lax.top_k(e_logits, TOP_K)
    gate = jax.nn.softmax(top_v, axis=-1) * p_sel
    expert = (g_sel[:, None] * EXPERTS_PER_GROUP + top_i).reshape(-1).astype(jnp.int32)
    token = jnp.repeat(jnp.arange(n_tok, dtype=jnp.int32), TOP_K)
    weight = gate.reshape(-1)
    n_asg = n_tok * TOP_K
    order = jnp.argsort(expert)
    s_exp, s_tok, s_w = expert[order], token[order], weight[order]
    counts = jnp.bincount(expert, length=N_EXPERTS)
    padded = (counts + EXPERT_BLOCK - 1) // EXPERT_BLOCK * EXPERT_BLOCK
    pad_end = jnp.cumsum(padded)
    slot = (pad_end - padded)[s_exp] + jnp.arange(n_asg, dtype=jnp.int32) - (jnp.cumsum(counts) - counts)[s_exp]
    n_blocks = -(-(n_asg + N_EXPERTS * (EXPERT_BLOCK - 1)) // EXPERT_BLOCK)
    slot_tok = jnp.full((n_blocks * EXPERT_BLOCK,), n_tok, jnp.int32).at[slot].set(s_tok)
    block_exp = jnp.minimum(jnp.searchsorted(pad_end, jnp.arange(n_blocks, dtype=jnp.int32) * EXPERT_BLOCK,
                                             side='right'), N_EXPERTS - 1)
    x_pad = jnp.concatenate([xt, jnp.zeros((1, dm), xt.dtype)], axis=0)

    def run_block(args):
        tok, e = args
        xb = x_pad[tok]
        hb = jax.nn.silu(xb @ w_gate[e]) * (xb @ w_up[e])
        return hb @ w_down[e]

    y_blocks = lax.map(run_block, (slot_tok.reshape(n_blocks, EXPERT_BLOCK), block_exp))
    y_slots = y_blocks.reshape(-1, dm)[slot].astype(F32)
    y = jax.ops.segment_sum(y_slots * s_w[:, None], s_tok, num_segments=n_tok)
    return y.astype(xn.dtype).reshape(bn, seq_len, dm)

def setup_inputs(seed: int = 0) -> dict:
    key = jax.random.key(seed)
    ks = jax.random.split(key, 24)
    nrm = lambda k, shape, scale: jax.random.normal(k, shape, F32) * scale
    gains = lambda k, shape: 1.0 + nrm(k, shape, 0.02)
    gate_b = jnp.stack([nrm(ks[6], (DEPTH, M_HEADS), 0.1),
                        jnp.linspace(3.0, 6.0, M_HEADS, dtype=F32) + nrm(ks[7], (DEPTH, M_HEADS), 0.1)], axis=1)
    return {
        "x": nrm(ks[0], (BATCH, SEQ, D_MODEL), 1.0),
        "meta_tokens": nrm(ks[1], (N_META, D_MODEL), 1.0),
        "norm1_g": gains(ks[2], (DEPTH, D_MODEL)),
        "w_in": nrm(ks[3], (DEPTH, D_MODEL, IN_WIDTH), D_MODEL ** -0.5),
        "conv_w": nrm(ks[4], (DEPTH, CONV_K, 2 * M_WIDTH), CONV_K ** -0.5),
        "conv_b": nrm(ks[5], (DEPTH, 2 * M_WIDTH), 0.02),
        "gate_b": gate_b,
        "m_norm_g": gains(ks[8], (DEPTH, M_WIDTH)),
        "a_w2": nrm(ks[9], (DEPTH, G_RANK, G_K_WIDTH), G_RANK ** -0.5),
        "a_b": nrm(ks[10], (DEPTH, G_K_WIDTH), 0.1),
        "g_norm_g": gains(ks[11], (DEPTH, G_WIDTH)),
        "w_out": nrm(ks[12], (DEPTH, MIX_WIDTH, D_MODEL), MIX_WIDTH ** -0.5),
        "norm2_g": gains(ks[13], (DEPTH, D_MODEL)),
        "wr_g": nrm(ks[14], (DEPTH, D_MODEL, N_GROUPS), D_MODEL ** -0.5),
        "br_g": nrm(ks[15], (DEPTH, N_GROUPS), 0.01),
        "wr_e": nrm(ks[16], (DEPTH, D_MODEL, N_EXPERTS), D_MODEL ** -0.5),
        "br_e": nrm(ks[17], (DEPTH, N_EXPERTS), 0.01),
        "w_gate": nrm(ks[18], (DEPTH, N_EXPERTS, D_MODEL, D_EXPERT), D_MODEL ** -0.5),
        "w_up": nrm(ks[19], (DEPTH, N_EXPERTS, D_MODEL, D_EXPERT), D_MODEL ** -0.5),
        "w_down": nrm(ks[20], (DEPTH, N_EXPERTS, D_EXPERT, D_MODEL), D_EXPERT ** -0.5),
        "final_norm_g": gains(ks[21], (D_MODEL,)),
    }

def reference(x, meta_tokens, norm1_g, w_in, conv_w, conv_b, gate_b, m_norm_g, a_w2, a_b, g_norm_g, w_out,
              norm2_g, wr_g, br_g, wr_e, br_e, w_gate, w_up, w_down, final_norm_g):
    bn = x.shape[0]
    meta = jnp.broadcast_to(meta_tokens[None].astype(x.dtype), (bn, N_META, x.shape[-1]))
    h = jnp.concatenate([meta, x], axis=1)
    for l in range(DEPTH):
        h = h + hybrid_mixer(rmsnorm(h, norm1_g[l]), w_in[l], conv_w[l], conv_b[l], gate_b[l], m_norm_g[l],
                             a_w2[l], a_b[l], g_norm_g[l], w_out[l])
        h = h + hierarchical_moe(rmsnorm(h, norm2_g[l]), wr_g[l], br_g[l], wr_e[l], br_e[l],
                                 w_gate[l], w_up[l], w_down[l])
    return rmsnorm(h, final_norm_g)[:, N_META:]


_drawn_inputs = setup_inputs


def setup_inputs(seed=0):
    import zlib

    import numpy as np

    out = dict(_drawn_inputs(seed))
    spreads = {}
    factors = {'conv_b': 4.298,
     'm_norm_g': 12.048,
     'g_norm_g': 9.703,
     'br_g': 64.0,
     'br_e': 19.248,
     'final_norm_g': 7.541,
     'norm2_g': 4.149}
    for name, (base, spread) in spreads.items():
        noise = np.random.default_rng([zlib.crc32(name.encode()), seed]).standard_normal(out[name].shape)
        drawn = base * np.exp(spread * noise) if base else spread * noise
        out[name] = __import__('jax').numpy.asarray(drawn.astype(out[name].dtype))
    for name, factor in factors.items():
        out[name] = (out[name] * factor).astype(out[name].dtype)
    return out
```

```python
import math
from contextlib import ExitStack

import concourse.bass as bass
from concourse import mybir

D_MODEL, SEQ, N_META = 1024, 2048, 16
EPS = 1e-6
M_HEADS, M_DIM, CONV_K = 4, 128, 4
G_HEADS, G_V, G_K, G_RANK, G_TAU = 4, 128, 64, 16, 16.0
M_WIDTH, G_WIDTH, G_KW = M_HEADS * M_DIM, G_HEADS * G_V, G_HEADS * G_K
N_GROUPS, PER_GROUP = 4, 8
N_EXPERTS = N_GROUPS * PER_GROUP
TOP_K, D_EXPERT = 2, 256

P = 128
KT = D_MODEL // P
CHUNKS = 1 + SEQ // P
PAD = P - N_META
TILES = SEQ // P

C_QK = 0
C_V = 2 * M_WIDTH
C_O = C_V + M_WIDTH
C_GATES = C_O + M_WIDTH
C_QG = C_GATES + 2 * M_HEADS
C_KG = C_QG + G_KW
C_VG = C_KG + G_KW
C_GG = C_VG + G_WIDTH
C_CODE = C_GG + G_WIDTH
IN_WIDTH = C_CODE + G_RANK
MISC = 2 * M_HEADS + G_RANK

LN_QK = math.log(M_DIM ** -0.5 / 4)
LEVELS = [64, 32, 16, 8, 4, 2, 1]
NEG = -1e30
SLOTS = 4
RING = 4
BLOCKS = (SEQ * TOP_K + N_EXPERTS * (P - 1)) // P + 3
FULL_BLOCKS = SEQ * TOP_K // P
ZERO_BLOCKS = BLOCKS - 2 - FULL_BLOCKS
LEVEL_BANKS = [(6, 7), (3, 5)]

R_NORM1, R_CONVW = 0, KT
R_CONVB = R_CONVW + CONV_K * KT
R_AB = R_CONVB + KT
R_MG = R_AB + G_KW // P
R_GG = R_MG + M_WIDTH // P
R_ALL = R_GG + G_WIDTH // P

F32 = mybir.dt.float32
I32 = mybir.dt.int32
U8 = mybir.dt.uint8
ALU = mybir.AluOpType
ACT = mybir.ActivationFunctionType
AX = mybir.AxisListType


def wait(eng, sem, value):
    if not (isinstance(value, int) and value <= 0):
        eng.wait_ge(sem, value)


def at(dram, index):
    if isinstance(index, int):
        return dram[index]
    return dram[bass.ds(index, 1)].rearrange("o p c -> (o p) c")


def mixer_phase(nc, t, vec, ident, mhalf, eps_col):
    ctx = ExitStack()
    with ctx:
        def sb(name, shape, dt=F32):
            return ctx.enter_context(nc.sbuf_tensor(name, shape, dt))

        def sem(name):
            return ctx.enter_context(nc.semaphore(name))

        w_in = sb("w_in_sb", [P, KT, IN_WIDTH])
        a_w2 = sb("a_w2_sb", [G_RANK, G_KW])
        gate_bi = sb("gate_bi", [M_HEADS, 1])
        gate_bf = sb("gate_bf", [M_HEADS, 1])
        x_in = sb("x_in", [P, D_MODEL])
        xn = sb("xn", [P, D_MODEL])
        xss = sb("xss", [P, 1])
        xms = sb("xms", [P, 1])
        xrs = sb("xrs", [P, 1])
        xnT = sb("xnT", [P, KT, P])
        conv_in = [sb(f"conv_in{p}", [P, KT, CONV_K - 1 + P]) for p in range(2)]
        v_aug = [sb(f"v_aug{p}", [P, M_HEADS, M_DIM + 1]) for p in range(2)]
        o_th = [sb(f"o_th{p}", [P, M_WIDTH]) for p in range(2)]
        qg = [sb(f"qg{p}", [P, 2, P]) for p in range(2)]
        kg = [sb(f"kg{p}", [P, 2, P]) for p in range(2)]
        vg = [sb(f"vg{p}", [P, G_WIDTH]) for p in range(2)]
        gate2 = [sb(f"gate2{p}", [P, G_WIDTH]) for p in range(2)]
        misc = [sb(f"misc{p}", [P, MISC]) for p in range(2)]
        acc = sb("conv_acc", [P, KT, P])
        cth = sb("conv_tanh", [P, KT, P])
        qkT = sb("qkT", [P, KT, P])
        codeT = sb("codeT", [G_RANK, P])
        rows = {n: sb("row_" + n, [M_HEADS, P]) for n in
                ("fg", "ig", "ig2", "l", "lf", "b", "c", "a", "winter", "floor", "wk")}
        m_row = [sb(f"m_row{p}", [M_HEADS, P]) for p in range(2)]
        cols = sb("cols", [P, 3 * M_HEADS])
        dec = sb("dec", [P, M_HEADS])
        em = sb("em", [P, M_HEADS, P])
        pT = sb("pT", [P, M_HEADS, P])
        qs = sb("qs", [P, M_HEADS, P])
        kw = sb("kw", [P, M_HEADS, P])
        c_st = sb("c_state", [P, M_HEADS, M_DIM + 1])
        r4 = sb("r4", [P, M_HEADS])
        ri4 = sb("ri4", [P, M_HEADS])
        gx = sb("gx", [P, 2, P])
        gl = sb("gl", [P, 2, P])
        gb = sb("gb", [P, 2, P])
        bend = sb("bend", [P, 2])
        eb = sb("eb", [P, 2, P])
        ebe = sb("ebe", [P, 2, P])
        qi = sb("qi", [P, 2, P])
        ki = sb("ki", [P, 2, P])
        xl = sb("xl", [P, len(LEVELS), 2, P])
        khat = sb("khat", [P, 2 * P])
        aT = sb("aT", [P, G_HEADS, P])
        s_st = sb("s_state", [P, 2, G_V])
        sq = qs[:, :, :].rearrange("p a b -> p (a b)")
        ss8 = sb("ss8", [P, M_HEADS + G_HEADS])
        ms8 = sb("ms8", [P, M_HEADS + G_HEADS])
        rs8 = sb("rs8", [P, M_HEADS + G_HEADS])
        cmask = sb("cmask", [P, P])
        lmask = sb("lmask", [P, len(LEVELS) + 1, P], U8)
        sel = sb("sel", [M_HEADS, M_HEADS, P])
        ones_gk = sb("ones_gk", [P, P])
        y = acc[:, :, :].rearrange("p a b -> p (a b)")
        yT = cth
        lmask_f = em[:, 0, :]
        vrows = em[0:R_ALL, 1, :]
        bank = [ctx.enter_context(nc.psum_tensor(f"bank{i}", [P, 512], F32)) for i in range(8)]

        w_loaded = [sem(f"w_loaded{i}") for i in range(8)]
        vec_loaded, small_loaded = sem("vec_loaded"), sem("small_loaded")
        vec_T, vec_ready = sem("vec_T"), sem("vec_ready")
        consts, consts_v, x_zeroed = sem("consts"), sem("consts_v"), sem("x_zeroed")
        x_loaded, x_ss, x_rs, xn_ready = sem("x_loaded"), sem("x_ss"), sem("x_rs"), sem("xn_ready")
        xT_ready, xnT_ready = sem("xT_ready"), sem("xnT_ready")
        q_ready, q_out, k_ready, k_out = sem("q_ready"), sem("q_out"), sem("k_ready"), sem("k_out")
        qkg_ready, qkg_out = sem("qkg_ready"), sem("qkg_out")
        v_ready, v_out, o_ready, o_out = sem("v_ready"), sem("v_out"), sem("o_ready"), sem("o_out")
        vg_ready, vg_out = sem("vg_ready"), sem("vg_out")
        gg_ready, gg_tanh, gate_done = sem("gg_ready"), sem("gg_tanh"), sem("gate_done")
        misc_ready, misc_out = sem("misc_ready"), sem("misc_out")
        gT_ready, gates_x, codeT_out = sem("gT_ready"), sem("gates_x"), sem("codeT_out")
        la_ready, gx_ready = sem("la_ready"), sem("gx_ready")
        ln_m, ln_g = sem("ln_m"), sem("ln_g")
        rows_ready, rows_exp = sem("rows_ready"), sem("rows_exp")
        conv_done, conv_tanh, qkT_ready = sem("conv_done"), sem("conv_tanh_s"), sem("qkT_ready")
        gb_ready, eb_ready, diff_ready, ediff_ready = sem("gb_ready"), sem("eb_ready"), sem("diff_ready"), sem("ediff_ready")
        qi_ready, kgt_ready, khat_out = sem("qi_ready"), sem("kgt_ready"), sem("khat_out")
        bc_ready, cols_ready, em_in, qs_ready, em_exp = (sem("bc_ready"), sem("cols_ready"), sem("em_in"),
                                                         sem("qs_ready"), sem("em_exp"))
        st_ready, pT_ready, kT_ready, kw_ready = sem("st_ready"), sem("pT_ready"), sem("kT_ready"), sem("kw_ready")
        xl_ready, lvl_ready, lvl_done = sem("xl_ready"), sem("lvl_ready"), sem("lvl_done")
        num_ready, h_ready, cu_ready, c_done = sem("num_ready"), sem("h_ready"), sem("cu_ready"), sem("c_done")
        og_ready, su_ready, s_done = sem("og_ready"), sem("su_ready"), sem("s_done")
        sqm_ready, sqg_ready, ss_ready, rs_ready = sem("sqm_ready"), sem("sqg_ready"), sem("ss_ready"), sem("rs_ready")
        og_used, y_ready, yT_ready, yT_out, yT_stored = (sem("og_used"), sem("y_ready"), sem("yT_ready"),
                                                         sem("yT_out"), sem("yT_stored"))
        act_seq, dve_seq, pool_seq = sem("act_seq"), sem("dve_seq"), sem("pool_seq")

        block = ctx.enter_context(nc.Block())
        N_LOOP = (CHUNKS - 3) // 2

        def chunk_program(eng, mix):
            mix(0, 0)
            with eng.Fori(0, N_LOOP) as j:
                for p in range(2):
                    mix(j * 2 + (1 + p), 1 - p)
            mix(CHUNKS - 2, (CHUNKS - 2) % 2)
            mix(CHUNKS - 1, (CHUNKS - 1) % 2)

        def is_last(c):
            return isinstance(c, int) and c == CHUNKS - 1

        W_PARTS = [(C_QK, C_QK + M_WIDTH), (C_QK + M_WIDTH, C_V), (C_QG, C_VG), (C_V, C_O), (C_O, C_GATES),
                   (C_VG, C_GG), (C_GG, C_CODE)]

        @block.sync
        def _(sp):
            sp.wait_ge(x_zeroed, 1)
            sp.dma_start(x_in[PAD:P, :], t["meta_tokens"]).then_inc(x_loaded, 16)
            n = 0
            for src, row in ((t["norm1_g"], R_NORM1), (t["conv_w"], R_CONVW), (t["conv_b"], R_CONVB),
                             (t["a_b"], R_AB), (t["m_norm_g"], R_MG), (t["g_norm_g"], R_GG)):
                count = src.shape[0] * src.shape[1] // P
                sp.dma_start(vrows[row:row + count, :], src.rearrange("a (k p) -> (a k) p", p=P)).then_inc(vec_loaded, 16)
                n += 1
            sp.dma_start(gate_bi[:, :], t["gate_b"][0:1, :].rearrange("o h -> h o")).then_inc(small_loaded, 16)
            sp.dma_start(gate_bf[:, :], t["gate_b"][1:2, :].rearrange("o h -> h o")).then_inc(small_loaded, 16)
            sp.dma_start(a_w2[:, :], t["a_w2"]).then_inc(small_loaded, 16)
            w_rows = t["w_in"].rearrange("(k p) n -> p k n", p=P)
            for i, (lo, hi) in enumerate(W_PARTS):
                sp.dma_start(w_in[:, :, lo:hi], w_rows[:, :, lo:hi]).then_inc(w_loaded[i], 16)
            sp.dma_start(w_in[:, :, C_GATES:C_QG], w_rows[:, :, C_GATES:C_QG]).then_inc(w_loaded[7], 16)
            sp.dma_start(w_in[:, :, C_CODE:IN_WIDTH], w_rows[:, :, C_CODE:IN_WIDTH]).then_inc(w_loaded[7], 16)
            sp.wait_ge(xn_ready, 1)
            sp.dma_start(x_in[:, :], at(t["x"], 0)).then_inc(x_loaded, 16)

            def mix(c, par):
                if not (isinstance(c, int) and c + 2 >= CHUNKS):
                    sp.wait_ge(xn_ready, c + 2)
                    sp.dma_start(x_in[:, :], at(t["x"], c + 1)).then_inc(x_loaded, 16)
                sp.wait_ge(yT_out, c + 1)
                sp.dma_start(at(t["yT"], c), yT[:, :, :].rearrange("p a b -> p (a b)")).then_inc(yT_stored, 16)

            chunk_program(sp, mix)
            sp.wait_ge(yT_stored, 16 * CHUNKS)

        @block.gpsimd
        def _(pool):
            n = [0]

            def link(ins):
                n[0] += 1
                ins.then_inc(pool_seq, 1)
                pool.wait_ge(pool_seq, n[0])

            pool.memset(x_in[:, :], 0.0).then_inc(x_zeroed, 1)
            link(pool.memset(ident[:, :], 0.0))
            link(pool.affine_select(out=ident[:, :], in_=ident[:, :], compare_op=ALU.not_equal, fill=1.0, base=0,
                                    pattern=[[-1, P]], channel_multiplier=1))
            link(pool.memset(xn[:, :], 0.0))
            link(pool.memset(mhalf[:, :], -0.5))
            link(pool.memset(eps_col[:, :], EPS))
            link(pool.memset(cmask[:, :], 0.0))
            link(pool.affine_select(out=cmask[:, :], in_=cmask[:, :], compare_op=ALU.is_ge, fill=NEG, base=0,
                                    pattern=[[1, P]], channel_multiplier=-1))
            for i, half in enumerate(LEVELS):
                size = 2 * half
                m = lmask_f.rearrange("p (b h r) -> p b h r", h=2, r=half)
                link(pool.memset(lmask_f, 0.0))
                link(pool.memset(m[:, :, 1, :], 1.0))
                link(pool.affine_select(out=lmask_f.rearrange("p (b r) -> p b r", r=size),
                                        in_=lmask_f.rearrange("p (b r) -> p b r", r=size), compare_op=ALU.is_ge,
                                        fill=0.0, base=0, pattern=[[-size, P // size], [0, size]], channel_multiplier=1))
                link(pool.affine_select(out=lmask_f.rearrange("p (b r) -> p b r", r=size),
                                        in_=lmask_f.rearrange("p (b r) -> p b r", r=size), compare_op=ALU.is_ge,
                                        fill=0.0, base=half - 1, pattern=[[size, P // size], [0, size]],
                                        channel_multiplier=-1))
                link(pool.tensor_copy(lmask[:, i, :], lmask_f))
            link(pool.tensor_copy(lmask[:, len(LEVELS), :], ident[:, :]))
            for h in range(M_HEADS):
                link(pool.tensor_copy(sel[:, h, :], ident[0:M_HEADS, h:h + 1].to_broadcast([M_HEADS, P])))
            pool.memset(aT[:, :, :], 0.0).then_inc(consts, 1)

            def x_power(m):
                pool.wait_ge(x_ss, m + 1)
                pool.tensor_tensor(xms[:, :], xss[:, :], eps_col[:, :], ALU.add).then_inc(pool_seq, 1)
                n[0] += 1
                pool.wait_ge(pool_seq, n[0])
                pool.tensor_tensor(xrs[:, :], xms[:, :], mhalf[:, 0:1], ALU.pow).then_inc(x_rs, 1)

            x_power(0)
            x_power(1)

            def mix(c, par):
                if not (isinstance(c, int) and c + 2 >= CHUNKS):
                    x_power(c + 2)
                pool.wait_ge(ss_ready, c + 1)
                pool.tensor_tensor(rs8[:, :], ms8[:, :], mhalf[:, :], ALU.pow).then_inc(rs_ready, 1)
                pool.sem_clear(pool_seq)
                n[0] = 0

            pool.sem_clear(pool_seq)
            n[0] = 0
            chunk_program(pool, mix)

        @block.scalar
        def _(act):
            n = [0]

            def link(ins):
                n[0] += 1
                ins.then_inc(act_seq, 1)
                act.wait_ge(act_seq, n[0])

            def x_norm(m):
                act.wait_ge(x_loaded, 16 * (m + 1))
                if not isinstance(m, int) or m > 0:
                    act.wait_ge(xT_ready, m)
                nc.scalar.activation(xn[:, :], x_in[:, :], ACT.Square, scale=D_MODEL ** -0.5,
                                     accum_out=xss[:, :]).then_inc(x_ss, 1)
                act.wait_ge(x_rs, m + 1)
                act.wait_ge(x_ss, m + 1)
                nc.scalar.activation(xn[:, :], x_in[:, :], ACT.Copy, scale=xrs[:, :]).then_inc(xn_ready, 1)

            def out_q(m, par):
                act.wait_ge(q_ready, m + 1)
                nc.scalar.activation(conv_in[par][:, 0:4, CONV_K - 1:], bank[0][:, :].rearrange("p (a b) -> p a b", a=4),
                                     ACT.Copy).then_inc(q_out, 1)

            def out_k(m, par):
                act.wait_ge(k_ready, m + 1)
                nc.scalar.activation(conv_in[par][:, 4:8, CONV_K - 1:], bank[1][:, :].rearrange("p (a b) -> p a b", a=4),
                                     ACT.Copy).then_inc(k_out, 1)

            def out_qkg(m, par):
                act.wait_ge(qkg_ready, m + 1)
                b = bank[0][:, :].rearrange("p (a b) -> p a b", a=4)
                nc.scalar.activation(qg[par][:, :, :], b[:, 0:2, :], ACT.Copy, scale=G_K ** -0.5).then_inc(act_seq, 1)
                n[0] += 1
                nc.scalar.activation(kg[par][:, :, :], b[:, 2:4, :], ACT.Copy).then_inc(qkg_out, 1)

            def out_v(m, par):
                act.wait_ge(v_ready, m + 1)
                nc.scalar.activation(v_aug[par][:, :, 0:M_DIM], bank[1][:, :].rearrange("p (a b) -> p a b", a=4),
                                     ACT.Copy).then_inc(v_out, 1)

            def out_o(m, par):
                act.wait_ge(o_ready, m + 1)
                nc.scalar.activation(o_th[par][:, :], bank[0][:, :], ACT.Tanh, scale=0.5).then_inc(o_out, 1)

            def out_vg(m, par):
                act.wait_ge(vg_ready, m + 1)
                nc.scalar.activation(vg[par][:, :], bank[1][:, :], ACT.Copy).then_inc(vg_out, 1)

            def out_gg(m, par):
                act.wait_ge(gg_ready, m + 1)
                nc.scalar.activation(gate2[par][:, :], bank[0][:, :], ACT.Tanh, scale=0.5).then_inc(gg_tanh, 1)

            def out_misc(m, par):
                act.wait_ge(misc_ready, m + 1)
                nc.scalar.activation(misc[par][:, :], bank[4][:, 0:MISC], ACT.Copy).then_inc(misc_out, 1)

            act.wait_ge(consts, 1)
            x_norm(0)
            for f in (out_q, out_k, out_qkg, out_v, out_o, out_vg, out_gg, out_misc):
                f(0, 0)
            x_norm(1)

            def mix(c, par):
                last, nxt = is_last(c), 1 - par
                act.wait_ge(gates_x, c + 1)
                link(nc.scalar.activation(rows["l"][:, :], rows["fg"][:, :], ACT.Abs))
                link(nc.scalar.activation(rows["l"][:, :], rows["l"][:, :], ACT.Exp, scale=-1.0))
                act.wait_ge(gx_ready, c + 1)
                link(nc.scalar.activation(gl[:, :, :], gx[:, :, :], ACT.Abs))
                link(nc.scalar.activation(gl[:, :, :], gl[:, :, :], ACT.Exp, scale=-1.0))
                nc.scalar.activation(rows["l"][:, :], rows["l"][:, :], ACT.Ln, bias=1.0).then_inc(ln_m, 1)
                nc.scalar.activation(gl[:, :, :], gl[:, :, :], ACT.Ln, bias=1.0).then_inc(ln_g, 1)
                act.wait_ge(rows_ready, c + 1)
                link(nc.scalar.activation(rows["winter"][:, :], rows["c"][:, :], ACT.Exp, bias=m_row[nxt][:, P - 1:P]))
                link(nc.scalar.activation(rows["floor"][:, :], m_row[par][:, :], ACT.Exp, scale=-1.0))
                nc.scalar.activation(rows["wk"][:, :], rows["a"][:, :], ACT.Exp,
                                     bias=rows["c"][:, P - 1:P]).then_inc(rows_exp, 1)
                act.wait_ge(gb_ready, c + 1)
                link(nc.scalar.activation(eb[:, :, :], gb[:, :, :], ACT.Exp, scale=1 / G_TAU))
                for j in range(2):
                    e = nc.scalar.activation(ebe[:, j, :], gb[:, j, :], ACT.Exp, scale=-1 / G_TAU, bias=bend[:, j:j + 1])
                    if j == 0:
                        link(e)
                e.then_inc(eb_ready, 1)
                act.wait_ge(diff_ready, c + 1)
                link(nc.scalar.activation(xl[:, :, :, :], xl[:, :, :, :], ACT.Abs))
                nc.scalar.activation(xl[:, :, :, :], xl[:, :, :, :], ACT.Exp, scale=-1 / G_TAU).then_inc(ediff_ready, 1)
                act.wait_ge(conv_done, c + 1)
                if not isinstance(c, int) or c > 0:
                    act.wait_ge(yT_stored, 16 * c)
                nc.scalar.activation(cth[:, :, :], acc[:, :, :], ACT.Tanh, scale=0.5).then_inc(conv_tanh, 1)
                if not last:
                    link(nc.scalar.activation(conv_in[nxt][:, :, 0:CONV_K - 1], conv_in[par][:, :, P:], ACT.Copy))
                    out_q(c + 1, nxt)
                    out_k(c + 1, nxt)
                act.wait_ge(em_in, c + 1)
                act.wait_ge(cols_ready, c + 1)
                for h in range(M_HEADS):
                    e = nc.scalar.activation(em[:, h, :], em[:, h, :], ACT.Exp, bias=cols[:, h:h + 1])
                    if h < M_HEADS - 1:
                        link(e)
                e.then_inc(em_exp, 1)
                act.wait_ge(kgt_ready, c + 1)
                nc.scalar.activation(khat[:, :], bank[5][:, 0:2 * P], ACT.Copy).then_inc(khat_out, 1)
                if not last:
                    out_qkg(c + 1, nxt)
                    if not (isinstance(c, int) and c + 2 >= CHUNKS):
                        x_norm(c + 2)
                    out_v(c + 1, nxt)
                act.wait_ge(h_ready, c + 1)
                nc.scalar.activation(sq, y[:, 0:M_WIDTH], ACT.Square).then_inc(sqm_ready, 1)
                if not last:
                    out_o(c + 1, nxt)
                act.wait_ge(og_ready, c + 1)
                for odd in range(2):
                    e = nc.scalar.activation(em[:, odd::2, :], bank[6 + odd][:, 0:2 * P].rearrange("p (a b) -> p a b", a=2),
                                             ACT.Square)
                    if odd == 0:
                        link(e)
                e.then_inc(sqg_ready, 1)
                if not last:
                    out_vg(c + 1, nxt)
                    out_gg(c + 1, nxt)
                    out_misc(c + 1, nxt)
                act.wait_ge(yT_ready, c + 1)
                for half in range(2):
                    e = nc.scalar.activation(yT[:, 4 * half:4 * half + 4, :],
                                             bank[2 + half][:, :].rearrange("p (a b) -> p a b", a=4), ACT.Copy)
                    if half == 0:
                        link(e)
                e.then_inc(yT_out, 1)
                act.wait_ge(act_seq, n[0])
                act.sem_clear(act_seq)
                n[0] = 0

            act.wait_ge(act_seq, n[0])
            act.sem_clear(act_seq)
            n[0] = 0
            chunk_program(act, mix)

        @block.tensor
        def _(pe):
            def channels(dst, col, tiles):
                for i in range(tiles):
                    for k in range(KT):
                        mm = nc.tensor.matmul(dst[:, i * P:(i + 1) * P], w_in[:, k, col + i * P:col + (i + 1) * P],
                                              xnT[:, k, :], start=(k == 0), stop=(k == KT - 1))
                return mm

            def tokens(dst, col, width):
                for k in range(KT):
                    mm = nc.tensor.matmul(dst, xnT[:, k, :], w_in[:, k, col:col + width],
                                          start=(k == 0), stop=(k == KT - 1))
                return mm

            def x_T(m):
                pe.wait_ge(xn_ready, m + 1)
                for k in range(KT):
                    b = bank[2 + k // 4]
                    mm = nc.tensor.transpose(b[:, (k % 4) * P:(k % 4 + 1) * P], xn[:, k * P:(k + 1) * P], ident[:, :])
                mm.then_inc(xT_ready, 1)

            def first(m, i):
                if isinstance(m, int) and m == 0:
                    pe.wait_ge(w_loaded[i], 16 if i < 7 else 32)

            def p_q(m):
                first(m, 0)
                pe.wait_ge(xnT_ready, m + 1)
                wait(pe, gate_done, m)
                channels(bank[0], C_QK, 4).then_inc(q_ready, 1)

            def p_k(m):
                first(m, 1)
                wait(pe, vg_out, m)
                channels(bank[1], C_QK + M_WIDTH, 4).then_inc(k_ready, 1)

            def p_qkg(m):
                first(m, 2)
                pe.wait_ge(q_out, m + 1)
                channels(bank[0], C_QG, 4).then_inc(qkg_ready, 1)

            def p_v(m):
                first(m, 3)
                pe.wait_ge(k_out, m + 1)
                tokens(bank[1][:, :], C_V, M_WIDTH).then_inc(v_ready, 1)

            def p_o(m):
                first(m, 4)
                pe.wait_ge(qkg_out, m + 1)
                tokens(bank[0][:, :], C_O, M_WIDTH).then_inc(o_ready, 1)

            def p_vg(m):
                first(m, 5)
                pe.wait_ge(v_out, m + 1)
                tokens(bank[1][:, :], C_VG, G_WIDTH).then_inc(vg_ready, 1)

            def p_gg(m):
                first(m, 6)
                pe.wait_ge(o_out, m + 1)
                tokens(bank[0][:, :], C_GG, G_WIDTH).then_inc(gg_ready, 1)

            def p_misc(m):
                first(m, 7)
                wait(pe, c_done, m)
                tokens(bank[4][:, 0:2 * M_HEADS], C_GATES, 2 * M_HEADS)
                tokens(bank[4][:, 2 * M_HEADS:MISC], C_CODE, G_RANK).then_inc(misc_ready, 1)

            pe.wait_ge(consts, 1)
            pe.wait_ge(vec_loaded, 16 * 6)
            nc.tensor.transpose(bank[7][:, 0:R_ALL], vrows, ident[0:R_ALL, 0:R_ALL]).then_inc(vec_T, 1)
            x_T(0)
            for f in (p_q, p_k, p_qkg, p_v, p_o, p_vg, p_gg, p_misc):
                f(0)
            pe.wait_ge(small_loaded, 48)
            pe.wait_ge(consts_v, 1)

            def mix(c, par):
                last = is_last(c)
                pe.wait_ge(misc_out, c + 1)
                nc.tensor.transpose(bank[4][0:M_HEADS, 0:P], misc[par][:, 0:M_HEADS], ident[:, :])
                nc.tensor.transpose(bank[4][0:M_HEADS, P:2 * P], misc[par][:, M_HEADS:2 * M_HEADS], ident[:, :])
                nc.tensor.transpose(bank[4][0:G_RANK, 2 * P:3 * P], misc[par][:, 2 * M_HEADS:], ident[:, :]).then_inc(gT_ready, 1)
                if not last:
                    wait(pe, yT_out, c)
                    x_T(c + 1)
                pe.wait_ge(codeT_out, c + 1)
                wait(pe, h_ready, c)
                for j in range(2):
                    mm = nc.tensor.matmul(bank[5][:, j * P:(j + 1) * P], a_w2[:, j * P:(j + 1) * P], codeT[:, :],
                                          start=True, stop=True)
                mm.then_inc(la_ready, 1)
                if not last:
                    p_q(c + 1)
                    p_k(c + 1)
                pe.wait_ge(rows_exp, c + 1)
                pe.wait_ge(gx_ready, c + 1)
                wait(pe, og_used, c)
                for h in range(M_HEADS):
                    nc.tensor.matmul(bank[6][:, h * P:(h + 1) * P], sel[:, h, :], rows["c"][:, :], start=True, stop=True)
                for h in range(M_HEADS):
                    nc.tensor.matmul(bank[7][:, h * P:(h + 1) * P], sel[:, h, :], rows["winter"][:, :], start=True, stop=True)
                for i, r in enumerate(("a", "floor", "wk")):
                    mm = nc.tensor.transpose(bank[5][:, 2 * P + 4 * i:2 * P + 4 * i + 4], rows[r][:, :],
                                             ident[0:M_HEADS, 0:M_HEADS])
                mm.then_inc(bc_ready, 1)
                pe.wait_ge(qkT_ready, c + 1)
                for h in range(M_HEADS):
                    mm = nc.tensor.matmul(bank[4][:, h * P:(h + 1) * P], qkT[:, M_HEADS + h, :], qkT[:, h, :],
                                          start=True, stop=True)
                mm.then_inc(st_ready, 1)
                if not last:
                    pe.wait_ge(xnT_ready, c + 2)
                else:
                    pe.wait_ge(yT_out, c)
                for h in range(M_HEADS):
                    mm = nc.tensor.transpose(bank[2][:, h * P:(h + 1) * P], qkT[:, M_HEADS + h, :], ident[:, :])
                mm.then_inc(kT_ready, 1)
                pe.wait_ge(qi_ready, c + 1)
                pe.wait_ge(cols_ready, c + 1)
                for j in range(2):
                    mm = nc.tensor.transpose(bank[5][:, j * P:(j + 1) * P], ki[:, j, :], ident[:, :])
                mm.then_inc(kgt_ready, 1)
                if not last:
                    p_qkg(c + 1)
                pe.wait_ge(xl_ready, c + 1)
                pe.wait_ge(em_in, c + 1)
                pe.wait_ge(qs_ready, c + 1)
                pe.wait_ge(khat_out, c + 1)
                for i in range(len(LEVELS) + 1):
                    pair, half = LEVEL_BANKS[i // 2 % 2], i % 2
                    if i // 2 >= 2 and half == 0:
                        pe.wait_ge(lvl_done, i // 2 - 1)
                    for h in range(G_HEADS):
                        part = slice(G_K * (h % 2), G_K * (h % 2) + G_K)
                        if i < len(LEVELS):
                            k_side = q_side = xl[part, i, h // 2, :]
                        else:
                            k_side, q_side = kg[par][part, h // 2, :], qg[par][part, h // 2, :]
                        col = (2 * half + h // 2) * P
                        mm = nc.tensor.matmul(bank[pair[h % 2]][:, col:col + P], k_side, q_side, start=True, stop=True)
                    if half == 1:
                        mm.then_inc(lvl_ready, 1)
                    if i == 3 and not last:
                        p_v(c + 1)
                pe.wait_ge(lvl_done, (len(LEVELS) + 1) // 2)
                pe.sem_clear(lvl_done)
                pe.wait_ge(pT_ready, c + 1)
                wait(pe, c_done, c)
                for h in range(M_HEADS):
                    dst = bank[3 + 2 * (h // 2)][:, (h % 2) * 256:(h % 2) * 256 + M_DIM + 1]
                    nc.tensor.matmul(dst, pT[:, h, :], v_aug[par][:, h, :], start=True, stop=False)
                    mm = nc.tensor.matmul(dst, qs[:, h, :], c_st[:, h, :], start=False, stop=True)
                mm.then_inc(num_ready, 1)
                pe.wait_ge(kw_ready, c + 1)
                for h in range(M_HEADS):
                    dst = bank[4 - 2 * (h // 2)][:, (h % 2) * 256:(h % 2) * 256 + M_DIM + 1]
                    mm = nc.tensor.matmul(dst, kw[:, h, :], v_aug[par][:, h, :], start=True, stop=True)
                mm.then_inc(cu_ready, 1)
                if not last:
                    p_o(c + 1)
                wait(pe, s_done, c)
                for h in range(G_HEADS):
                    part = slice(G_K * (h % 2), G_K * (h % 2) + G_K)
                    dst = bank[6 + h % 2][:, (h // 2) * P:(h // 2 + 1) * P]
                    nc.tensor.matmul(dst, aT[:, h, :], vg[par][:, h * P:(h + 1) * P], start=True, stop=False)
                    mm = nc.tensor.matmul(dst, qi[part, h // 2, :], s_st[part, h // 2, :], start=False, stop=True)
                mm.then_inc(og_ready, 1)
                pe.wait_ge(h_ready, c + 1)
                for j in range(2):
                    mm = nc.tensor.matmul(bank[3][:, j * 2 * P:(j + 1) * 2 * P], khat[:, j * P:(j + 1) * P],
                                          vg[par][:, j * 2 * P:(j + 1) * 2 * P], start=True, stop=True)
                mm.then_inc(su_ready, 1)
                if not last:
                    p_vg(c + 1)
                    p_gg(c + 1)
                    p_misc(c + 1)
                pe.wait_ge(y_ready, c + 1)
                pe.wait_ge(c_done, c + 1)
                pe.wait_ge(s_done, c + 1)
                for k in range(KT):
                    mm = nc.tensor.transpose(bank[2 + k // 4][:, (k % 4) * P:(k % 4 + 1) * P], y[:, k * P:(k + 1) * P],
                                             ident[:, :])
                mm.then_inc(yT_ready, 1)

            chunk_program(pe, mix)

        @block.vector
        def _(v):
            n = [0]

            def step(ins):
                n[0] += 1
                ins.then_inc(dve_seq, 1)

            def settle():
                v.wait_ge(dve_seq, n[0])

            def link(ins):
                step(ins)
                settle()

            v.wait_ge(vec_T, 1)
            nc.vector.tensor_copy(vec[:, :], bank[7][:, 0:R_ALL]).then_inc(vec_ready, 1)
            v.wait_ge(vec_ready, 1)
            step(nc.vector.memset(c_st[:, :, :], 0.0))
            step(nc.vector.memset(s_st[:, :, :], 0.0))
            step(nc.vector.memset(m_row[1][:, :], 0.0))
            step(nc.vector.memset(ones_gk[:, :], 1.0))
            step(nc.vector.memset(conv_in[0][:, :, 0:CONV_K - 1], 0.0))
            for p in range(2):
                step(nc.vector.memset(v_aug[p][:, :, M_DIM:M_DIM + 1], 1.0))
            settle()
            nc.vector.memset(bend[:, :], 0.0).then_inc(consts_v, 1)
            v.wait_ge(consts_v, 1)
            v.wait_ge(small_loaded, 48)

            def out_xT(m):
                v.wait_ge(xT_ready, m + 1)
                wait(v, misc_ready, m)
                for half in range(2):
                    g = vec[:, R_NORM1 + 4 * half:R_NORM1 + 4 * half + 4]
                    e = nc.vector.tensor_tensor(xnT[:, 4 * half:4 * half + 4, :],
                                                bank[2 + half][:, :].rearrange("p (a b) -> p a b", a=4),
                                                g.unsqueeze(2).to_broadcast([P, 4, P]), ALU.mult)
                    if half == 0:
                        step(e)
                e.then_inc(xnT_ready, 1)

            def out_gate(m, par):
                v.wait_ge(gg_tanh, m + 1)
                nc.vector.scalar_tensor_tensor(gate2[par][:, :], gate2[par][:, :], 1.0, bank[0][:, :],
                                               ALU.add, ALU.mult).then_inc(gate_done, 1)

            out_xT(0)
            out_gate(0, 0)

            def mix(c, par):
                last, nxt = is_last(c), 1 - par
                head0 = isinstance(c, int) and c == 0
                v.wait_ge(gT_ready, c + 1)
                nc.vector.tensor_copy(codeT[:, :], bank[4][0:G_RANK, 2 * P:3 * P]).then_inc(codeT_out, 1)
                step(nc.vector.tensor_scalar(rows["ig"][:, :], bank[4][0:M_HEADS, 0:P], gate_bi[:, :], None, ALU.add))
                step(nc.vector.tensor_scalar(rows["ig2"][:, :], bank[4][0:M_HEADS, 0:P], gate_bi[:, :], LN_QK,
                                             ALU.add, ALU.add))
                if head0:
                    settle()
                    step(nc.vector.memset(rows["ig"][:, 0:PAD], NEG))
                    step(nc.vector.memset(rows["ig2"][:, 0:PAD], NEG))
                nc.vector.tensor_scalar(rows["fg"][:, :], bank[4][0:M_HEADS, P:2 * P], gate_bf[:, :], None,
                                        ALU.add).then_inc(gates_x, 1)
                if not last:
                    out_xT(c + 1)
                v.wait_ge(la_ready, c + 1)
                for j in range(2):
                    e = nc.vector.tensor_scalar(gx[:, j, :], bank[5][:, j * P:(j + 1) * P],
                                                vec[:, R_AB + j:R_AB + j + 1], None, ALU.add)
                    if j == 0:
                        step(e)
                e.then_inc(gx_ready, 1)
                v.wait_ge(k_out, c + 1)
                wait(v, yT_ready, c)
                for j in range(CONV_K):
                    for i in range(KT):
                        w = vec[:, R_CONVW + j * KT + i:R_CONVW + j * KT + i + 1]
                        src = conv_in[par][:, i, j:j + P]
                        if j == 0:
                            e = nc.vector.tensor_scalar(acc[:, i, :], src, w, vec[:, R_CONVB + i:R_CONVB + i + 1],
                                                        ALU.mult, ALU.add)
                        else:
                            e = nc.vector.scalar_tensor_tensor(acc[:, i, :], src, w, acc[:, i, :], ALU.mult, ALU.add)
                        if (j, i) != (CONV_K - 1, KT - 1):
                            step(e)
                    if j < CONV_K - 1:
                        settle()
                e.then_inc(conv_done, 1)
                v.wait_ge(ln_m, c + 1)
                link(nc.vector.scalar_tensor_tensor(rows["lf"][:, :], rows["fg"][:, :], 0.0, rows["l"][:, :],
                                                    ALU.min, ALU.subtract))
                if head0:
                    link(nc.vector.memset(rows["lf"][:, 0:PAD], 0.0))
                step(nc.vector.tensor_tensor_scan(rows["b"][:, :], ones_gk[0:M_HEADS, :], rows["lf"][:, :], 0.0,
                                                  ALU.mult, ALU.add))
                link(nc.vector.tensor_tensor_scan(m_row[par][:, :], rows["lf"][:, :], rows["ig"][:, :],
                                                  m_row[nxt][:, P - 1:P], ALU.add, ALU.max))
                step(nc.vector.tensor_tensor(rows["a"][:, :], rows["ig2"][:, :], rows["b"][:, :], ALU.subtract))
                nc.vector.tensor_tensor(rows["c"][:, :], rows["b"][:, :], m_row[par][:, :],
                                        ALU.subtract).then_inc(rows_ready, 1)
                v.wait_ge(ln_g, c + 1)
                link(nc.vector.scalar_tensor_tensor(gx[:, :, :], gx[:, :, :], 0.0, gl[:, :, :], ALU.min, ALU.subtract))
                for j in range(2):
                    step(nc.vector.tensor_tensor_scan(gb[:, j, :], ones_gk[:, :], gx[:, j, :], 0.0, ALU.mult, ALU.add))
                settle()
                nc.vector.tensor_scalar(bend[:, :], gb[:, :, P - 1], 1 / G_TAU, None, ALU.mult).then_inc(gb_ready, 1)
                for i, half in enumerate(LEVELS):
                    size = 2 * half
                    g = gb[:, :, :].rearrange("p j (b r) -> p j b r", r=size)
                    e = nc.vector.tensor_tensor(xl[:, i, :, :].rearrange("p j (b r) -> p j b r", r=size), g,
                                                g[:, :, :, half - 1:half].to_broadcast([P, 2, P // size, size]),
                                                ALU.subtract)
                    if i < len(LEVELS) - 1:
                        step(e)
                e.then_inc(diff_ready, 1)
                v.wait_ge(conv_tanh, c + 1)
                nc.vector.scalar_tensor_tensor(qkT[:, :, :], cth[:, :, :], 1.0, acc[:, :, :],
                                               ALU.add, ALU.mult).then_inc(qkT_ready, 1)
                v.wait_ge(eb_ready, c + 1)
                step(nc.vector.tensor_tensor(ki[:, :, :], kg[par][:, :, :], ebe[:, :, :], ALU.mult))
                nc.vector.tensor_tensor(qi[:, :, :], qg[par][:, :, :], eb[:, :, :], ALU.mult).then_inc(qi_ready, 1)
                v.wait_ge(bc_ready, c + 1)
                nc.vector.tensor_copy(cols[:, :], bank[5][:, 2 * P:2 * P + 3 * M_HEADS]).then_inc(cols_ready, 1)
                nc.vector.tensor_tensor(em[:, :, :], bank[6][:, :].rearrange("p (a b) -> p a b", a=4),
                                        cmask[:, :].unsqueeze(1).to_broadcast([P, M_HEADS, P]), ALU.add).then_inc(em_in, 1)
                w4 = bank[7][:, :].rearrange("p (a b) -> p a b", a=4)
                step(nc.vector.tensor_copy(dec[:, :], w4[:, :, P - 1]))
                v.wait_ge(qkT_ready, c + 1)
                nc.vector.tensor_tensor(qs[:, :, :], w4, qkT[:, 0:M_HEADS, :], ALU.mult).then_inc(qs_ready, 1)
                v.wait_ge(kT_ready, c + 1)
                v.wait_ge(cols_ready, c + 1)
                nc.vector.tensor_tensor(kw[:, :, :], bank[2][:, :].rearrange("p (a b) -> p a b", a=4),
                                        cols[:, 2 * M_HEADS:].unsqueeze(2).to_broadcast([P, M_HEADS, P]),
                                        ALU.mult).then_inc(kw_ready, 1)
                v.wait_ge(ediff_ready, c + 1)
                for i, half in enumerate(LEVELS):
                    for side, src in ((0, kg), (1, qg)):
                        xv = xl[:, i, :, :].rearrange("p j (b h r) -> p j b h r", h=2, r=half)[:, :, :, side, :]
                        sv = src[par][:, :, :].rearrange("p j (b h r) -> p j b h r", h=2, r=half)[:, :, :, side, :]
                        e = nc.vector.tensor_tensor(xv, xv, sv, ALU.mult)
                        if (i, side) != (len(LEVELS) - 1, 1):
                            step(e)
                e.then_inc(xl_ready, 1)
                v.wait_ge(st_ready, c + 1)
                v.wait_ge(em_exp, c + 1)
                nc.vector.tensor_tensor(pT[:, :, :], bank[4][:, :].rearrange("p (a b) -> p a b", a=4), em[:, :, :],
                                        ALU.mult).then_inc(pT_ready, 1)
                for i in range(len(LEVELS) + 1):
                    pair, half = LEVEL_BANKS[i // 2 % 2], i % 2
                    if half == 0:
                        v.wait_ge(lvl_ready, i // 2 + 1)
                    settle()
                    for odd in range(2):
                        e = nc.vector.copy_predicated(
                            aT[:, odd::2, :], lmask[:, i, :].unsqueeze(1).to_broadcast([P, 2, P]),
                            bank[pair[odd]][:, 2 * half * P:2 * (half + 1) * P].rearrange("p (a b) -> p a b", a=2))
                        if half == 1 and odd == 1:
                            e.then_inc(lvl_done, 1)
                        else:
                            step(e)
                    if half == 1 and i < len(LEVELS):
                        v.wait_ge(lvl_done, i // 2 + 1)
                v.sem_clear(lvl_ready)
                v.wait_ge(num_ready, c + 1)
                den = [bank[3 + 2 * b][:, :].rearrange("p (a b) -> p a b", a=2)[:, :, M_DIM] for b in range(2)]
                for b in range(2):
                    step(nc.vector.scalar_tensor_tensor(r4[:, 2 * b:2 * b + 2], den[b], -1.0,
                                                        cols[:, M_HEADS + 2 * b:M_HEADS + 2 * b + 2], ALU.mult, ALU.max))
                settle()
                for b in range(2):
                    step(nc.vector.tensor_tensor(r4[:, 2 * b:2 * b + 2], den[b], r4[:, 2 * b:2 * b + 2], ALU.max))
                settle()
                link(nc.vector.reciprocal(ri4[:, :], r4[:, :]))
                for b in range(2):
                    e = nc.vector.tensor_tensor(
                        y[:, b * 256:(b + 1) * 256].rearrange("p (a b) -> p a b", a=2),
                        bank[3 + 2 * b][:, :].rearrange("p (a b) -> p a b", a=2)[:, :, 0:M_DIM],
                        ri4[:, 2 * b:2 * b + 2].unsqueeze(2).to_broadcast([P, 2, M_DIM]), ALU.mult)
                    if b == 0:
                        step(e)
                e.then_inc(h_ready, 1)
                v.wait_ge(cu_ready, c + 1)
                for h in range(M_HEADS):
                    src = bank[4 - 2 * (h // 2)][:, (h % 2) * 256:(h % 2) * 256 + M_DIM + 1]
                    e = nc.vector.scalar_tensor_tensor(c_st[:, h, :], c_st[:, h, :], dec[:, h:h + 1], src,
                                                       ALU.mult, ALU.add)
                    if h < M_HEADS - 1:
                        step(e)
                e.then_inc(c_done, 1)
                v.wait_ge(sqm_ready, c + 1)
                step(nc.vector.tensor_reduce(ss8[:, 0:M_HEADS], sq.rearrange("p (a b) -> p a b", a=4), axis=AX.X,
                                             op=ALU.add))
                v.wait_ge(sqg_ready, c + 1)
                link(nc.vector.tensor_reduce(ss8[:, M_HEADS:], em[:, :, :], axis=AX.X, op=ALU.add))
                nc.vector.tensor_scalar(ms8[:, :], ss8[:, :], 4.0 / M_DIM, 4.0 * EPS, ALU.mult, ALU.add).then_inc(ss_ready, 1)
                v.wait_ge(su_ready, c + 1)
                for h in range(G_HEADS):
                    part, j = slice(G_K * (h % 2), G_K * (h % 2) + G_K), h // 2
                    e = nc.vector.scalar_tensor_tensor(s_st[part, j, :], s_st[part, j, :], eb[part, j, P - 1:P],
                                                       bank[3][part, h * P:(h + 1) * P], ALU.mult, ALU.add)
                    if h < G_HEADS - 1:
                        step(e)
                e.then_inc(s_done, 1)
                v.wait_ge(rs_ready, c + 1)
                v.wait_ge(h_ready, c + 1)
                ym = y[:, 0:M_WIDTH].rearrange("p (a b) -> p a b", a=4)
                yg = y[:, M_WIDTH:].rearrange("p (a b) -> p a b", a=4)
                for odd in range(2):
                    e = nc.vector.tensor_tensor(yg[:, odd::2, :], bank[6 + odd][:, 0:2 * P].rearrange("p (a b) -> p a b", a=2),
                                                rs8[:, M_HEADS + odd::2].unsqueeze(2).to_broadcast([P, 2, P]), ALU.mult)
                    if odd == 0:
                        step(e)
                e.then_inc(og_used, 1)
                link(nc.vector.tensor_tensor(ym, ym, rs8[:, 0:M_HEADS].unsqueeze(2).to_broadcast([P, 4, P]), ALU.mult))
                step(nc.vector.scalar_tensor_tensor(y[:, 0:M_WIDTH], o_th[par][:, :], 1.0, y[:, 0:M_WIDTH],
                                                    ALU.add, ALU.mult))
                v.wait_ge(og_used, c + 1)
                nc.vector.tensor_tensor(y[:, M_WIDTH:], y[:, M_WIDTH:], gate2[par][:, :], ALU.mult).then_inc(y_ready, 1)
                if not last:
                    out_gate(c + 1, nxt)
                settle()
                v.sem_clear(dve_seq)
                n[0] = 0

            settle()
            v.sem_clear(dve_seq)
            n[0] = 0
            chunk_program(v, mix)



def router_phase(nc, t, c, h_all, logits):
    ctx = ExitStack()
    with ctx:
        def sb(name, shape, dt=F32):
            return ctx.enter_context(nc.sbuf_tensor(name, shape, dt))

        def sem(name):
            return ctx.enter_context(nc.semaphore(name))

        w_out = sb("w_out_sb", [P, KT, D_MODEL])
        wr = sb("wr", [P, KT, N_GROUPS + N_EXPERTS])
        br = sb("br", [P, N_GROUPS + N_EXPERTS])
        yT = [sb(f"yT_in{p}", [P, KT, P]) for p in range(2)]
        h = [sb(f"h{p}", [P, D_MODEL]) for p in range(2)]
        xn = [sb(f"xn2_{p}", [P, KT, P]) for p in range(2)]
        xT = sb("xn2T", [P, KT, P])
        sq = sb("sq2", [P, D_MODEL])
        ss, ms, rs = sb("ss2", [P, 1]), sb("ms2", [P, 1]), sb("rs2", [P, 1])
        zeros = sb("zeros", [P, D_MODEL])
        zeroed, zeros_stored = sem("zeroed"), sem("zeros_stored")
        bank = [ctx.enter_context(nc.psum_tensor(f"rbank{i}", [P, 512], F32)) for i in range(8)]

        w_loaded, w_scaled, r_loaded, g_loaded = sem("wout_loaded"), sem("wout_scaled"), sem("wr_loaded"), sem("g2_loaded")
        y_loaded = [sem(f"y_loaded{p}") for p in range(2)]
        x_loaded = [sem(f"x2_loaded{p}") for p in range(2)]
        xn_stored = [sem(f"xn2_stored{p}") for p in range(2)]
        o_ready, h_ready, h_kept = sem("o2_ready"), sem("h2_ready"), sem("h2_kept")
        ss_ready, rs_ready, xn_ready = sem("ss2_ready"), sem("rs2_ready"), sem("xn2_ready")
        xT_ready, xT_out, lg_ready, lg_out = sem("x2T_ready"), sem("x2T_out"), sem("lg_ready"), sem("lg_out")
        dve_seq, pool_seq = sem("dve_seq2"), sem("pool_seq2")
        block = ctx.enter_context(nc.Block())

        def tiles(eng, body):
            with eng.Fori(0, TILES // 2 - 1) as j:
                for p in range(2):
                    body(j * 2 + p, j, p)
            for p in range(2):
                body(TILES - 2 + p, TILES // 2 - 1, p)

        @block.sync
        def _(sp):
            sp.dma_start(yT[0][:, :, :].rearrange("p a b -> p (a b)"), at(t["yT"], 1)).then_inc(y_loaded[0], 16)
            sp.dma_start(w_out[:, :, :], t["w_out"].rearrange("(k p) n -> p k n", p=P)).then_inc(w_loaded, 16)
            sp.dma_start(wr[:, :, 0:N_GROUPS], t["wr_g"].rearrange("(p k) n -> p k n", k=KT)).then_inc(r_loaded, 16)
            sp.dma_start(wr[:, :, N_GROUPS:], t["wr_e"].rearrange("(p k) n -> p k n", k=KT)).then_inc(r_loaded, 16)
            sp.dma_start(br[:, 0:N_GROUPS], t["br_g"].partition_broadcast(P)).then_inc(r_loaded, 16)
            sp.dma_start(br[:, N_GROUPS:], t["br_e"].partition_broadcast(P)).then_inc(r_loaded, 16)
            sp.dma_start(c["g2"][:, :], t["norm2_g"].rearrange("o (p k) -> (o p) k", k=KT)).then_inc(g_loaded, 16)
            sp.dma_start(c["gf"][:, :], t["final_norm_g"].partition_broadcast(P)).then_inc(g_loaded, 16)
            sp.dma_start(h[0][:, :], at(t["x"], 0)).then_inc(x_loaded[0], 16)

            sp.dma_start(yT[1][:, :, :].rearrange("p a b -> p (a b)"), at(t["yT"], 2)).then_inc(y_loaded[1], 16)
            sp.dma_start(h[1][:, :], at(t["x"], 1)).then_inc(x_loaded[1], 16)

            sp.wait_ge(zeroed, 1)

            def body(i, j, p):
                for k in range(ZERO_BLOCKS // TILES):
                    sp.dma_start(at(t["y_slots"], i * (ZERO_BLOCKS // TILES) + (FULL_BLOCKS + k)),
                                 zeros[:, :]).then_inc(zeros_stored, 16)
                sp.wait_ge(xn_ready, i + 1)
                sp.dma_start(at(t["xn2"], i), xn[p][:, :, :].rearrange("p a b -> p (a b)")).then_inc(xn_stored[p], 16)
                if not (isinstance(i, int) and i >= TILES - 2):
                    sp.wait_ge(o_ready, i + 1)
                    sp.dma_start(yT[p][:, :, :].rearrange("p a b -> p (a b)"), at(t["yT"], i + 3)).then_inc(y_loaded[p], 16)
                    sp.wait_ge(h_kept, i + 1)
                    sp.dma_start(h[p][:, :], at(t["x"], i + 2)).then_inc(x_loaded[p], 16)

            tiles(sp, body)
            for p in range(2):
                sp.wait_ge(xn_stored[p], 16 * TILES // 2)
            sp.wait_ge(g_loaded, 32)
            sp.wait_ge(zeros_stored, 16 * ZERO_BLOCKS)

        @block.gpsimd
        def _(pool):
            pool.memset(zeros[:, :], 0.0).then_inc(zeroed, 1)

            def body(i, j, p):
                pool.wait_ge(ss_ready, i + 1)
                pool.tensor_tensor(ms[:, :], ss[:, :], c["eps_col"][:, :], ALU.add).then_inc(pool_seq, 1)
                pool.wait_ge(pool_seq, 1)
                pool.sem_clear(pool_seq)
                pool.tensor_tensor(rs[:, :], ms[:, :], c["mhalf"][:, 0:1], ALU.pow).then_inc(rs_ready, 1)

            tiles(pool, body)

        @block.scalar
        def _(act):
            def body(i, j, p):
                act.wait_ge(h_ready, i + 1)
                nc.scalar.activation(sq[:, :], h[p][:, :], ACT.Square, scale=D_MODEL ** -0.5,
                                     accum_out=ss[:, :]).then_inc(ss_ready, 1)
                act.wait_ge(rs_ready, i + 1)
                act.wait_ge(xn_stored[p], j * 16)
                act.wait_ge(xT_ready, i)
                nc.scalar.activation(xn[p][:, :, :], h[p][:, :].rearrange("t (p k) -> t k p", k=KT), ACT.Copy,
                                     scale=rs[:, :]).then_inc(xn_ready, 1)

            tiles(act, body)

        @block.tensor
        def _(pe):
            pe.wait_ge(w_scaled, 1)
            pe.wait_ge(r_loaded, 64)

            def project(i, j, p):
                pe.wait_ge(y_loaded[p], (j + 1) * 16)
                wait(pe, h_ready, i - 1)
                for n in range(2):
                    for k in range(KT):
                        mm = nc.tensor.matmul(bank[2 * p + n][:, :], yT[p][:, k, :], w_out[:, k, n * 512:(n + 1) * 512],
                                              start=(k == 0), stop=(k == KT - 1))
                mm.then_inc(o_ready, 1)

            def route(i, j, p):
                pe.wait_ge(xn_ready, i + 1)
                pe.wait_ge(xT_out, i)
                for k in range(KT):
                    mm = nc.tensor.transpose(bank[4 + k // 4][:, (k % 4) * P:(k % 4 + 1) * P], xn[p][:, k, :],
                                             c["ident"][:, :])
                mm.then_inc(xT_ready, 1)
                pe.wait_ge(xT_out, i + 1)
                pe.wait_ge(lg_out, i)
                for k in range(KT):
                    mm = nc.tensor.matmul(bank[6][:, 0:N_GROUPS + N_EXPERTS], xT[:, k, :], wr[:, k, :],
                                          start=(k == 0), stop=(k == KT - 1))
                mm.then_inc(lg_ready, 1)

            project(0, 0, 0)

            def body(i, j, p):
                if not (isinstance(i, int) and i == TILES - 1):
                    project(i + 1, j + p, 1 - p)
                route(i, j, p)

            tiles(pe, body)

        @block.vector
        def _(v):
            nc.vector.memset(c["zero"][:, :], 0.0).then_inc(dve_seq, 1)
            v.wait_ge(w_loaded, 16)
            for k in range(KT):
                e = nc.vector.tensor_scalar(w_out[:, k, :], w_out[:, k, :], c["vec"][:, R_MG + k:R_MG + k + 1], None, ALU.mult)
                if k < KT - 1:
                    e.then_inc(dve_seq, 1)
            e.then_inc(w_scaled, 1)
            v.wait_ge(dve_seq, KT)
            v.sem_clear(dve_seq)
            v.wait_ge(g_loaded, 32)

            def residual(i, j, p):
                v.wait_ge(o_ready, i + 1)
                v.wait_ge(x_loaded[p], (j + 1) * 16)
                nc.vector.tensor_tensor(h[p][:, 0:512], h[p][:, 0:512], bank[2 * p][:, :], ALU.add).then_inc(dve_seq, 1)
                nc.vector.tensor_tensor(h[p][:, 512:], h[p][:, 512:], bank[2 * p + 1][:, :], ALU.add).then_inc(h_ready, 1)
                v.wait_ge(dve_seq, 1)
                v.sem_clear(dve_seq)
                v.wait_ge(h_ready, i + 1)
                dst = h_all[:, i, :] if isinstance(i, int) else h_all[:, bass.ds(i, 1), :].rearrange("p o c -> p (o c)")
                nc.vector.tensor_tensor(dst, h[p][:, :],
                                        c["zero"][:, 0:1].to_broadcast([P, D_MODEL]), ALU.add).then_inc(h_kept, 1)

            def route(i, j, p):
                v.wait_ge(xT_ready, i + 1)
                v.wait_ge(lg_ready, i)
                for half in range(2):
                    e = nc.vector.tensor_tensor(xT[:, 4 * half:4 * half + 4, :],
                                                bank[4 + half][:, :].rearrange("p (a b) -> p a b", a=4),
                                                c["g2"][:, 4 * half:4 * half + 4].unsqueeze(2).to_broadcast([P, 4, P]), ALU.mult)
                    if half == 0:
                        e.then_inc(dve_seq, 1)
                e.then_inc(xT_out, 1)
                v.wait_ge(lg_ready, i + 1)
                dst = logits[:, i, :] if isinstance(i, int) else logits[:, bass.ds(i, 1), :].rearrange("p o c -> p (o c)")
                nc.vector.tensor_tensor(dst, bank[6][:, 0:N_GROUPS + N_EXPERTS], br[:, :], ALU.add).then_inc(lg_out, 1)
                v.wait_ge(dve_seq, 1)
                v.sem_clear(dve_seq)

            residual(0, 0, 0)

            def body(i, j, p):
                if not (isinstance(i, int) and i == TILES - 1):
                    residual(i + 1, j + p, 1 - p)
                route(i, j, p)

            tiles(v, body)
            v.wait_ge(lg_out, TILES)



def experts_phase(nc, t, c, h_all, logits):
    ctx = ExitStack()
    with ctx:
        def sb(name, shape, dt=F32):
            return ctx.enter_context(nc.sbuf_tensor(name, shape, dt))

        def sem(name):
            return ctx.enter_context(nc.semaphore(name))

        E, G, NT = N_EXPERTS, N_GROUPS, TILES
        w_size = KT * D_EXPERT
        w_all = sb("w_all", [P, SLOTS * 3 * KT, D_EXPERT])
        w_slot = w_all[:, :, :].rearrange("p (s m) f -> p s (m f)", s=SLOTS)
        xg_all, xT_all, y_all = sb("xg", [P, 2, D_MODEL]), sb("xgT", [P, 2, D_MODEL]), sb("yb", [P, 2, D_MODEL])
        xg = [xg_all[:, p, :].rearrange("q (a b) -> q a b", a=KT) for p in range(2)]
        xT = [xT_all[:, p, :].rearrange("q (a b) -> q a b", a=KT) for p in range(2)]
        sg = sb("silu_gate", [P, D_EXPERT])
        hid = [sb(f"hid{p}", [P, 2, P]) for p in range(2)]
        hidT = sb("hidT", [P, 2, P])
        yb = [y_all[:, p, :] for p in range(2)]
        iota_e = sb("iota_e", [P, E])
        iota_g = sb("iota_g", [P, G])
        iota_i = sb("iota_i", [P, E], I32)
        tok = sb("tok", [P, NT])
        tok_i = sb("tok_i", [P, NT], I32)
        tri = sb("tri", [P, P])
        ones = sb("ones", [P, P])
        work = y_all[:, :, :].rearrange("p a (b i e) -> p (a b) i e", b=2, e=E)
        oh = [work[:, i] for i in range(2)]
        lm, tmp = work[:, 2], work[:, 3]
        slotv = sb("slotv", [P, NT, E])
        ohg = sb("ohg", [P, NT, G])
        gt = sb("group_work", [P, NT, G])[:, :, :]
        mx = [sb(f"mx{i}", [P, NT]) for i in range(3)]
        idx1 = sb("idx1", [P, NT])
        wt = [sb(f"wt{i}", [P, NT]) for i in range(2)]
        ex = sb("ex", [P, NT])
        slot_f = [sb(f"slot_f{i}", [P, NT]) for i in range(2)]
        slot_i = [sb(f"slot_i{i}", [P, NT], I32) for i in range(2)]
        cnt = sb("cnt", [P, E])
        cnt_i = sb("cnt_i", [P, E], I32)
        pad_end = sb("pad_end", [P, E])
        start = sb("start", [P, E])
        NB = BLOCKS - 2
        blk_i = xg_all[0:1, :, :].rearrange("p a (b e) -> p (a b) e", e=E).bitcast(I32)
        blk = xT_all[0:1, :, :].rearrange("p a (b e) -> p (a b) e", e=E)
        exp_f = sb("exp_f", [1, NB])
        exp_i = sb("exp_i", [1, BLOCKS], I32)
        free_i = sb("free_i", [1, E], I32)
        nblk_i = sb("nblk_i", [1, 1], I32)
        zrow = sb("zrow", [BLOCKS, P])
        srow = sb("srow", [BLOCKS, P])
        sidT = sb("sidT", [P, BLOCKS])
        cur = [sb(f"cur{p}", [P, 1], I32) for p in range(2)]
        cur2 = [sb(f"cur2{p}", [P, 1], I32) for p in range(2)]
        zero_i = sb("zero_i", [P, 1], I32)
        zero_f = sb("zero_f", [P, 1])
        fsq = xg_all[:, 0, :]
        fss, fms, frs = sb("fss", [P, 1]), sb("fms", [P, 1]), sb("frs", [P, 2])
        bank = [ctx.enter_context(nc.psum_tensor(f"ebank{i}", [P, 512], F32)) for i in range(8)]

        w_loaded = [sem(f"expert_loaded{i}") for i in range(SLOTS)]
        consts, zeros_out, scattered, srow_loaded, sidT_ready = (sem("consts3"), sem("zeros_out"), sem("scattered"),
                                                                 sem("srow_loaded"), sem("sidT_ready"))
        tables, slots_ready, oh_ready, rank_ready, exm, exm_done = (sem("tables"), sem("slots_ready"), sem("oh_ready"),
                                                                    sem("rank_ready"), sem("exm"), sem("exm_done"))
        sid_out = sem("sid_out")
        cur_ready = sem("cur_ready")
        xg_loaded = [sem(f"xg_loaded{p}") for p in range(2)]
        xt_ready, xT_out, gu_ready, sg_ready, h_ready = (sem("xt_ready"), sem("xT_out3"), sem("gu_ready"),
                                                         sem("sg_ready"), sem("h_ready3"))
        ht_ready, hT_out, d_ready, ya_out, yb_out = sem("ht_ready"), sem("hT_out"), sem("d_ready"), sem("ya_out"), sem("yb_out")
        y_stored = [sem(f"y_stored{p}") for p in range(2)]
        got = [sem(f"got{r}") for r in range(RING)]
        sum_ready, fss_ready, frs_ready, o_ready = sem("sum_ready"), sem("fss_ready"), sem("frs_ready"), sem("o_ready3")
        o_stored = [sem(f"o_stored{r}") for r in range(RING)]
        dve_seq, pool_seq = sem("dve_seq3"), sem("pool_seq3")
        block = ctx.enter_context(nc.Block())

        def blocks(eng, body):
            n = eng.value_load(nblk_i[0:1, 0:1], min_val=SEQ * TOP_K // P, max_val=BLOCKS - 3)
            with eng.Fori(0, (BLOCKS - 2) // 2) as j:
                for q in range(2):
                    b = j * 2 + (1 + q)
                    with eng.If(b < n + 1):
                        body(b, j, 1 - q)
            return n

        @block.sync
        def _(sp):
            def load(e, s):
                def src(name, k):
                    w = t[name][e:e + 1] if isinstance(e, int) else t[name][bass.ds(e, 1)]
                    return w.rearrange("o (p k) f -> (o p) (k f)", k=k)
                for i, (name, k) in enumerate((("w_gate", KT), ("w_up", KT), ("w_down", D_EXPERT // P))):
                    sp.dma_start(w_slot[:, s, i * w_size:(i + 1) * w_size], src(name, k)).then_inc(w_loaded[s], 16)

            sp.wait_ge(consts, 1)
            sp.dma_start(t["slot_tok"].rearrange("(b p) o -> b (p o)", p=P), zrow[:, :]).then_inc(zeros_out, 16)
            for s in range(SLOTS):
                load(s, s)
            sp.wait_ge(scattered, 16 * 2 * NT)
            sp.dma_start(srow[:, :], t["slot_tok"].rearrange("(b p) o -> b (p o)", p=P)).then_inc(srow_loaded, 16)
            sp.wait_ge(tables, 1)
            with sp.Fori(1, E // SLOTS) as j:
                for s in range(SLOTS):
                    e = j * SLOTS + s
                    done = sp.value_load(free_i[0:1, bass.ds(e, 1)], min_val=0, max_val=BLOCKS)
                    sp.wait_ge(d_ready, done)
                    load(e, s)
            for i in range(NT):
                sp.wait_ge(o_ready, i + 1)
                sp.dma_start(t["out"][i], w_slot[:, i % RING, 0:D_MODEL]).then_inc(o_stored[i % RING], 16)
            for r in range(RING):
                sp.wait_ge(o_stored[r], 16 * (NT // RING))

        @block.gpsimd
        def _(pool):
            n = [0]

            def link(ins):
                n[0] += 1
                ins.then_inc(pool_seq, 1)
                pool.wait_ge(pool_seq, n[0])

            link(pool.memset(zrow[:, :], 0.0))
            link(pool.memset(zero_i[:, :], 0))
            link(pool.memset(zero_f[:, :], 0.0))
            link(pool.memset(ones[:, :], 1.0))
            link(pool.memset(tri[:, :], 1.0))
            link(pool.affine_select(out=tri[:, :], in_=tri[:, :], compare_op=ALU.is_ge, fill=0.0, base=-1,
                                    pattern=[[1, P]], channel_multiplier=-1))
            link(pool.iota(iota_i[:, :], pattern=[[1, E]], base=-E, channel_multiplier=0))
            link(pool.tensor_copy(iota_e[:, :], iota_i[:, :]))
            link(pool.iota(iota_i[:, 0:G], pattern=[[1, G]], base=-G, channel_multiplier=0))
            link(pool.tensor_copy(iota_g[:, :], iota_i[:, 0:G]))
            link(pool.iota(tok_i[:, :], pattern=[[P, NT]], base=0, channel_multiplier=1))
            link(pool.tensor_copy(tok[:, :], tok_i[:, :]))
            link(pool.iota(blk_i, pattern=[[1, NB], [0, E]], base=0, channel_multiplier=0))
            pool.tensor_copy(blk, blk_i).then_inc(consts, 1)
            pool.wait_ge(consts, 1)
            pool.wait_ge(zeros_out, 16)
            pool.wait_ge(slots_ready, 1)
            for i in range(NT):
                for k in range(TOP_K):
                    pool.indirect_dma_start(t["slot_tok"], bass.IndirectOffsetOnAxis(ap=slot_i[k][:, i:i + 1], axis=0),
                                            tok[:, i:i + 1], None).then_inc(scattered, 16)
            rows = t["xn2"].rearrange("i p c -> (i p) c")

            def gather(b, q):
                pool.wait_ge(cur_ready, b + 1)
                pool.tensor_tensor(cur2[q][:, :], cur[q][:, :], zero_i[:, :], ALU.add).then_inc(pool_seq, 1)
                pool.wait_ge(pool_seq, 1)
                pool.sem_clear(pool_seq)
                pool.indirect_dma_start(xg_all[:, q, :], None, rows,
                                        bass.IndirectOffsetOnAxis(ap=cur2[q][:, 0:1], axis=0)).then_inc(xg_loaded[q], 16)

            pool.sem_clear(pool_seq)
            gather(0, 0)
            gather(1, 1)

            def body(b, j, p):
                pool.wait_ge(xt_ready, b)
                gather(b + 1, 1 - p)

            nb = blocks(pool, body)
            y_rows = t["y_slots"].rearrange("b p c -> (b p) c")
            pool.wait_ge(d_ready, nb)
            for p in range(2):
                pool.wait_ge(y_stored[p], ((nb + (1 - p)) >> 1) * 16)
            pool.tensor_tensor(cur2[0][:, :], cur[0][:, :], zero_i[:, :], ALU.add).then_inc(pool_seq, 1)
            pool.wait_ge(pool_seq, 1)
            pool.sem_clear(pool_seq)

            def collect(i):
                r = i % RING
                if i >= RING:
                    pool.wait_ge(o_stored[r], 16 * (i // RING))
                for k in range(TOP_K):
                    pool.indirect_dma_start(w_slot[:, r, k * D_MODEL:(k + 1) * D_MODEL], None, y_rows,
                                            bass.IndirectOffsetOnAxis(ap=slot_i[k][:, i:i + 1], axis=0)).then_inc(got[r], 16)

            for i in range(RING - 1):
                collect(i)
            for i in range(NT):
                if i + RING - 1 < NT:
                    collect(i + RING - 1)
                pool.wait_ge(fss_ready, i + 1)
                pool.tensor_tensor(fms[:, :], fss[:, :], c["eps_col"][:, :], ALU.add).then_inc(pool_seq, 1)
                pool.wait_ge(pool_seq, i + 1)
                wait(pool, o_ready, i - 1)
                pool.tensor_tensor(frs[:, i % 2:i % 2 + 1], fms[:, :], c["mhalf"][:, 0:1], ALU.pow).then_inc(frs_ready, 1)

        @block.scalar
        def _(act):
            act.wait_ge(exm, 1)
            nc.scalar.activation(gt, gt, ACT.Exp).then_inc(exm_done, 1)
            act.wait_ge(exm, 2)
            nc.scalar.activation(ex[:, :], ex[:, :], ACT.Exp).then_inc(exm_done, 1)
            act.wait_ge(tables, 1)

            def silu(b, p):
                act.wait_ge(gu_ready, b + 1)
                wait(act, h_ready, b)
                nc.scalar.activation(sg[:, :], bank[2 + p][:, 0:D_EXPERT], ACT.Silu).then_inc(sg_ready, 1)

            silu(0, 0)

            def body(b, j, p):
                silu(b, p)
                act.wait_ge(ht_ready, b)
                act.wait_ge(d_ready, b - 1)
                nc.scalar.activation(hidT[:, :, :], bank[4][:, 0:2 * P].rearrange("p (a b) -> p a b", a=2),
                                     ACT.Copy).then_inc(hT_out, 1)
                act.wait_ge(d_ready, b)
                act.wait_ge(y_stored[1 - p], j * 16)
                nc.scalar.activation(yb[1 - p][:, 0:512], bank[5][:, :], ACT.Copy).then_inc(ya_out, 1)
                act.wait_ge(yb_out, b)
                act.wait_ge(ya_out, b)
                act.dma_start(at(t["y_slots"], b - 1), yb[1 - p][:, :]).then_inc(y_stored[1 - p], 16)

            blocks(act, body)
            for i in range(NT):
                act.wait_ge(sum_ready, i + 1)
                wait(act, frs_ready, i)
                nc.scalar.activation(fsq, w_slot[:, i % RING, 0:D_MODEL], ACT.Square, scale=D_MODEL ** -0.5,
                                     accum_out=fss[:, :]).then_inc(fss_ready, 1)

        @block.tensor
        def _(pe):
            pe.wait_ge(consts, 1)
            pe.wait_ge(oh_ready, 1)
            flat = lm.rearrange("p a b -> p (a b)")
            nc.tensor.matmul(bank[0][:, :], tri[:, :], flat, start=True, stop=True)
            nc.tensor.matmul(bank[1][:, :], ones[:, :], flat, start=True, stop=True).then_inc(rank_ready, 1)
            pe.wait_ge(srow_loaded, 16)
            pe.wait_ge(tables, 1)
            nc.tensor.transpose(bank[7][:, 0:BLOCKS], srow[:, :], c["ident"][0:BLOCKS, 0:BLOCKS]).then_inc(sidT_ready, 1)
            pe.wait_ge(sid_out, 1)

            def transpose_x(b, q, count):
                pe.wait_ge(xg_loaded[q], count)
                wait(pe, xT_out, b)
                for k in range(KT):
                    mm = nc.tensor.transpose(bank[k // 4][:, (k % 4) * P:(k % 4 + 1) * P], xg[q][:, k, :], c["ident"][:, :])
                mm.then_inc(xt_ready, 1)

            def gate_up(b, p):
                e = pe.value_load(exp_i[0:1, b:b + 1] if isinstance(b, int) else exp_i[0:1, bass.ds(b, 1)],
                                  min_val=0, max_val=E - 1)
                pe.wait_ge(xT_out, b + 1)
                wait(pe, h_ready, b - 1)
                for s in range(SLOTS):
                    pe.wait_ge(w_loaded[s], ((e + (SLOTS - s)) // SLOTS) * 48)
                slot = e % SLOTS
                for i in range(2):
                    for k in range(KT):
                        w = w_all[:, bass.ds(slot * (3 * KT) + (i * KT + k), 1), :].rearrange("p o f -> p (o f)")
                        mm = nc.tensor.matmul(bank[2 + p][:, i * D_EXPERT:(i + 1) * D_EXPERT], xT[p][:, k, :], w,
                                              start=(k == 0), stop=(k == KT - 1))
                mm.then_inc(gu_ready, 1)

            transpose_x(0, 0, 16)
            gate_up(0, 0)
            transpose_x(1, 1, 16)

            def body(b, j, p):
                gate_up(b, p)
                pe.wait_ge(h_ready, b)
                pe.wait_ge(hT_out, b - 1)
                for i in range(2):
                    mm = nc.tensor.transpose(bank[4][:, i * P:(i + 1) * P], hid[1 - p][:, i, :], c["ident"][:, :])
                mm.then_inc(ht_ready, 1)
                transpose_x(b + 1, 1 - p, (j + 2) * 16 if p == 1 else (j + 2) * 16)
                e = pe.value_load(exp_i[0:1, bass.ds(b - 1, 1)], min_val=0, max_val=E - 1)
                slot = e % SLOTS
                pe.wait_ge(hT_out, b)
                pe.wait_ge(ya_out, b - 1)
                pe.wait_ge(yb_out, b - 1)
                for half in range(2):
                    for i in range(2):
                        w = w_all[:, bass.ds(slot * (3 * KT) + (2 * KT + (i * D_MODEL + half * 512) // D_EXPERT), 2), :]
                        mm = nc.tensor.matmul(bank[5 + half][:, :], hidT[:, i, :], w.rearrange("p o f -> p (o f)"),
                                              start=(i == 0), stop=(i == 1))
                mm.then_inc(d_ready, 1)

            blocks(pe, body)

        @block.vector
        def _(v):
            n = [0]

            def step(ins):
                n[0] += 1
                ins.then_inc(dve_seq, 1)

            def settle():
                v.wait_ge(dve_seq, n[0])

            def link(ins):
                step(ins)
                settle()

            TT, TS, STT, RED = (nc.vector.tensor_tensor, nc.vector.tensor_scalar, nc.vector.scalar_tensor_tensor,
                                nc.vector.tensor_reduce)
            v.wait_ge(consts, 1)
            lg, le = logits[:, :, 0:G], logits[:, :, G:]

            def first_max(one_hot, values, m, work, iota, width):
                shape = [P, NT, width]
                link(RED(m[:, :], values, axis=AX.X, op=ALU.max))
                link(TT(work, values, m[:, :].unsqueeze(2).to_broadcast(shape), ALU.is_equal))
                link(TT(work, work, iota[:, :].unsqueeze(1).to_broadcast(shape), ALU.mult))
                link(RED(idx1[:, :], work, axis=AX.X, op=ALU.min))
                link(TT(one_hot, iota[:, :].unsqueeze(1).to_broadcast(shape), idx1[:, :].unsqueeze(2).to_broadcast(shape),
                        ALU.is_equal))

            first_max(ohg[:, :, :], lg, mx[0], gt, iota_g, G)
            TT(gt, lg, mx[0][:, :].unsqueeze(2).to_broadcast([P, NT, G]), ALU.subtract).then_inc(exm, 1)
            link(TS(ohg[:, :, :], ohg[:, :, :], -1.0, -NEG, ALU.add, ALU.mult))
            link(TT(lm.rearrange("p i (g e) -> p i g e", g=G), le.rearrange("p i (g e) -> p i g e", g=G),
                    ohg[:, :, :].unsqueeze(3).to_broadcast([P, NT, G, PER_GROUP]), ALU.add))
            first_max(oh[0], lm, mx[1], tmp, iota_e, E)
            link(STT(lm, oh[0], 3 * NEG, lm, ALU.mult, ALU.add))
            first_max(oh[1], lm, mx[2], tmp, iota_e, E)
            TT(lm, oh[0], oh[1], ALU.add).then_inc(oh_ready, 1)
            v.wait_ge(exm_done, 1)
            TT(ex[:, :], mx[2][:, :], mx[1][:, :], ALU.subtract).then_inc(exm, 1)
            link(RED(mx[0][:, :], gt, axis=AX.X, op=ALU.add))
            v.wait_ge(exm_done, 2)
            link(STT(wt[0][:, :], ex[:, :], 1.0, mx[0][:, :], ALU.add, ALU.mult))
            link(nc.vector.reciprocal(wt[0][:, :], wt[0][:, :]))
            link(TT(wt[1][:, :], wt[0][:, :], ex[:, :], ALU.mult))
            v.wait_ge(rank_ready, 1)
            tot = bank[1][:, :].rearrange("p (i e) -> p i e", i=NT)
            link(RED(cnt[:, :], bank[1][:, :].rearrange("p (i e) -> p e i", i=NT), axis=AX.X, op=ALU.add))
            link(TS(cnt_i[:, :], cnt[:, :], float(P - 1), None, ALU.add))
            link(TS(cnt_i[:, :], cnt_i[:, :], P.bit_length() - 1, None, ALU.arith_shift_right))
            link(nc.vector.tensor_copy(cnt[:, :], cnt_i[:, :]))
            link(nc.vector.tensor_tensor_scan(pad_end[:, :], ones[:, 0:E], cnt[:, :], 0.0, ALU.mult, ALU.add))
            link(TT(start[:, :], pad_end[:, :], cnt[:, :], ALU.subtract))
            link(TS(slotv[:, 0, :], start[:, :], float(P), None, ALU.mult))
            for i in range(NT - 1):
                link(TT(slotv[:, i + 1, :], slotv[:, i, :], tot[:, i, :], ALU.add))
            link(TT(slotv[:, :, :], slotv[:, :, :], bank[0][:, :].rearrange("p (i e) -> p i e", i=NT), ALU.add))
            for k in range(TOP_K):
                link(TT(tmp, oh[k], slotv[:, :, :], ALU.mult))
                link(RED(slot_f[k][:, :], tmp, axis=AX.X, op=ALU.add))
            link(nc.vector.tensor_copy(slot_i[0][:, :], slot_f[0][:, :]))
            nc.vector.tensor_copy(slot_i[1][:, :], slot_f[1][:, :]).then_inc(slots_ready, 1)
            link(TT(blk, blk, pad_end[0:1, :].unsqueeze(1).to_broadcast([1, NB, E]), ALU.is_ge))
            link(RED(exp_f[:, :], blk, axis=AX.X, op=ALU.add))
            link(nc.vector.memset(exp_i[:, NB:], 0))
            link(TS(exp_i[:, 0:NB], exp_f[:, :], float(E - 1), None, ALU.min))
            link(nc.vector.memset(free_i[:, 0:SLOTS], 0))
            link(nc.vector.tensor_copy(free_i[:, SLOTS:], pad_end[0:1, 0:E - SLOTS]))
            nc.vector.tensor_copy(nblk_i[:, :], pad_end[0:1, E - 1:E]).then_inc(tables, 1)
            v.wait_ge(tables, 1)
            v.wait_ge(sidT_ready, 1)
            nc.vector.tensor_copy(sidT[:, :], bank[7][:, 0:BLOCKS]).then_inc(sid_out, 1)
            v.wait_ge(sid_out, 1)
            v.sem_clear(dve_seq)
            n[0] = 0

            def index(b, q):
                src = sidT[:, b:b + 1] if isinstance(b, int) else sidT[:, bass.ds(b, 1)]
                TT(cur[q][:, :], src, zero_f[:, :], ALU.add).then_inc(cur_ready, 1)

            def out_x(b, q):
                v.wait_ge(xt_ready, b + 1)
                wait(v, gu_ready, b - 1)
                for half in range(2):
                    e = TT(xT[q][:, 4 * half:4 * half + 4, :], bank[half][:, :].rearrange("p (a b) -> p a b", a=4),
                           c["g2"][:, 4 * half:4 * half + 4].unsqueeze(2).to_broadcast([P, 4, P]), ALU.mult)
                    if half == 0:
                        e.then_inc(dve_seq, 1)
                e.then_inc(xT_out, 1)

            def hidden(b, p):
                v.wait_ge(sg_ready, b + 1)
                wait(v, ht_ready, b - 1)
                TT(hid[p][:, :, :], sg[:, :].rearrange("t (q j) -> t j q", j=2),
                   bank[2 + p][:, D_EXPERT:].rearrange("t (q j) -> t j q", j=2), ALU.mult).then_inc(h_ready, 1)

            index(0, 0)
            index(1, 1)
            out_x(0, 0)
            hidden(0, 0)
            out_x(1, 1)
            v.wait_ge(dve_seq, 2)
            v.sem_clear(dve_seq)

            def body(b, j, p):
                v.wait_ge(xg_loaded[1 - p], (j + 1) * 16)
                index(b + 1, 1 - p)
                hidden(b, p)
                out_x(b + 1, 1 - p)
                v.wait_ge(d_ready, b)
                v.wait_ge(y_stored[1 - p], j * 16)
                nc.vector.tensor_copy(yb[1 - p][:, 512:], bank[6][:, :]).then_inc(yb_out, 1)
                v.wait_ge(dve_seq, 1)
                v.sem_clear(dve_seq)

            blocks(v, body)
            for i in range(NT):
                r = i % RING
                a, b = w_slot[:, r, 0:D_MODEL], w_slot[:, r, D_MODEL:2 * D_MODEL]
                v.wait_ge(got[r], 32 * (i // RING + 1))
                link(STT(a, a, wt[0][:, i:i + 1], h_all[:, i, :], ALU.mult, ALU.add))
                STT(a, b, wt[1][:, i:i + 1], a, ALU.mult, ALU.add).then_inc(sum_ready, 1)
                if i:
                    finish(nc, v, c, w_slot, frs, frs_ready, o_ready, sum_ready, i - 1)
            finish(nc, v, c, w_slot, frs, frs_ready, o_ready, sum_ready, NT - 1)


def finish(nc, v, c, w_slot, frs, frs_ready, o_ready, sum_ready, i):
    a = w_slot[:, i % RING, 0:D_MODEL]
    v.wait_ge(frs_ready, i + 1)
    v.wait_ge(sum_ready, i + 1)
    nc.vector.scalar_tensor_tensor(a, a, frs[:, i % 2:i % 2 + 1], c["gf"][:, :], ALU.mult, ALU.mult).then_inc(o_ready, 1)


def build(nc, t):
    t = dict(t)
    t["yT"] = nc.dram_tensor("yT_dram", (CHUNKS, P, D_MODEL), F32).ap()
    t["xn2"] = nc.dram_tensor("xn2_dram", (TILES, P, D_MODEL), F32).ap()
    t["slot_tok"] = nc.dram_tensor("slot_tok", (BLOCKS * P, 1), F32).ap()
    t["y_slots"] = nc.dram_tensor("y_slots", (BLOCKS - 2, P, D_MODEL), F32).ap()
    ctx = ExitStack()
    with ctx:
        def sb(name, shape, dt=F32):
            return ctx.enter_context(nc.sbuf_tensor(name, shape, dt))

        c = {"vec": sb("vec", [P, R_ALL]), "ident": sb("ident", [P, P]), "mhalf": sb("mhalf", [P, M_HEADS + G_HEADS]),
             "eps_col": sb("eps_col", [P, 1])}
        mixer_phase(nc, t, c["vec"], c["ident"], c["mhalf"], c["eps_col"])
        h_all = sb("h_all", [P, TILES, D_MODEL])
        logits = sb("logits", [P, TILES, N_GROUPS + N_EXPERTS])
        c["g2"], c["gf"], c["zero"] = sb("g2", [P, KT]), sb("gf", [P, D_MODEL]), sb("zero", [P, 1])
        router_phase(nc, t, c, h_all, logits)
        experts_phase(nc, t, c, h_all, logits)


_WEIGHTS = ["norm1_g", "w_in", "conv_w", "conv_b", "gate_b", "m_norm_g", "a_w2", "a_b", "g_norm_g", "w_out", "norm2_g",
            "wr_g", "br_g", "wr_e", "br_e", "w_gate", "w_up", "w_down"]
_ROWS = {"norm1_g", "conv_b", "m_norm_g", "a_b", "g_norm_g", "norm2_g", "br_g", "br_e"}


def kernel(**inputs):
    import concourse.bacc as bacc
    import numpy as np
    from concourse.bass_utils import run_bass_kernel_spmd

    arrays = {"x": np.asarray(inputs["x"]).reshape(TILES, P, D_MODEL), "meta_tokens": np.asarray(inputs["meta_tokens"]),
              "final_norm_g": np.asarray(inputs["final_norm_g"])}
    for name in _WEIGHTS:
        a = np.asarray(inputs[name])
        arrays[name] = a if name in _ROWS else a[0]
    nc = bacc.Bacc("TRN2", target_bir_lowering=False, num_devices=1)
    t = {}
    for name, a in arrays.items():
        arrays[name] = np.ascontiguousarray(a)
        t[name] = nc.dram_tensor(name, a.shape, F32, kind="ExternalInput").ap()
    t["out"] = nc.dram_tensor("out", (TILES, P, D_MODEL), F32, kind="ExternalOutput").ap()
    build(nc, t)
    r = run_bass_kernel_spmd(nc, [arrays], core_ids=[0])
    return r.results[0]["out"].reshape(1, SEQ, D_MODEL)
```

```python
import math
from contextlib import ExitStack

import concourse.bass as bass
from concourse import mybir

D_MODEL, SEQ, N_META = 1024, 2048, 16
EPS = 1e-6
M_HEADS, M_DIM, CONV_K = 4, 128, 4
G_HEADS, G_V, G_K, G_RANK, G_TAU = 4, 128, 64, 16, 16.0
M_WIDTH, G_WIDTH, G_KW = M_HEADS * M_DIM, G_HEADS * G_V, G_HEADS * G_K
N_GROUPS, PER_GROUP = 4, 8
N_EXPERTS = N_GROUPS * PER_GROUP
TOP_K, D_EXPERT = 2, 256

P = 128
KT = D_MODEL // P
CHUNKS = 1 + SEQ // P
PAD = P - N_META
TILES = SEQ // P

C_QK = 0
C_V = 2 * M_WIDTH
C_O = C_V + M_WIDTH
C_GATES = C_O + M_WIDTH
C_QG = C_GATES + 2 * M_HEADS
C_KG = C_QG + G_KW
C_VG = C_KG + G_KW
C_GG = C_VG + G_WIDTH
C_CODE = C_GG + G_WIDTH
IN_WIDTH = C_CODE + G_RANK
MISC = 2 * M_HEADS + G_RANK

LN_QK = math.log(M_DIM ** -0.5 / 4)
LEVELS = [64, 32, 16, 8, 4, 2, 1]
NEG = -1e30
SLOTS = 4
RING = 4
BLOCKS = (SEQ * TOP_K + N_EXPERTS * (P - 1)) // P + 3
FULL_BLOCKS = SEQ * TOP_K // P
ZERO_BLOCKS = BLOCKS - 2 - FULL_BLOCKS
LEVEL_BANKS = [(6, 7), (3, 5)]

R_NORM1, R_CONVW = 0, KT
R_CONVB = R_CONVW + CONV_K * KT
R_AB = R_CONVB + KT
R_MG = R_AB + G_KW // P
R_GG = R_MG + M_WIDTH // P
R_ALL = R_GG + G_WIDTH // P

F32 = mybir.dt.float32
F32R = mybir.dt.float32r
I32 = mybir.dt.int32
U8 = mybir.dt.uint8
ALU = mybir.AluOpType
ACT = mybir.ActivationFunctionType
AX = mybir.AxisListType


def wait(eng, sem, value):
    if not (isinstance(value, int) and value <= 0):
        eng.wait_ge(sem, value)


def at(dram, index):
    if isinstance(index, int):
        return dram[index]
    return dram[bass.ds(index, 1)].rearrange("o p c -> (o p) c")


def place(nc, start, sizes):
    views, pos = {}, 0
    for name, size, dt in sizes:
        views[name] = nc.alloc_sbuf_tensor_at(name, [P, size], dt, offset=start + 4 * pos)[:, :]
        pos += size
    assert pos <= KT * IN_WIDTH
    return views


def router_views(nc, start):
    pairs = [(name + str(p), D_MODEL, dt) for name, dt in (("yT_", F32), ("h_", F32), ("y_hi", F32R), ("y_lo", F32R),
                                                           ("xn2_", F32)) for p in range(2)]
    views = place(nc, start, [("w_lo", KT * D_MODEL, F32R), ("w_hi", KT * D_MODEL, F32R)] + pairs +
                  [("squares", D_MODEL, F32), ("zeros", D_MODEL, F32)])
    views.update(place(nc, start, [("w_raw", KT * D_MODEL, F32)]))
    return views


def mixer_phase(nc, t, c_all):
    vec, ident, mhalf, eps_col = c_all["vec"], c_all["ident"], c_all["mhalf"], c_all["eps_col"]
    views = c_all["views"]
    ctx = ExitStack()
    with ctx:
        def sb(name, shape, dt=F32):
            return ctx.enter_context(nc.sbuf_tensor(name, shape, dt))

        def sem(name):
            return ctx.enter_context(nc.semaphore(name))

        w_in = c_all["region"][:, :].rearrange("p (k n) -> p k n", k=KT)
        a_w2 = sb("a_w2_sb", [G_RANK, G_KW])
        gate_bi = sb("gate_bi", [M_HEADS, 1])
        gate_bf = sb("gate_bf", [M_HEADS, 1])
        x_in = sb("x_in", [P, D_MODEL])
        xn = sb("xn", [P, D_MODEL])
        xss = sb("xss", [P, 1])
        xms = sb("xms", [P, 1])
        xrs = sb("xrs", [P, 1])
        xnT = sb("xnT", [P, KT, P])
        conv_in = [sb(f"conv_in{p}", [P, KT, CONV_K - 1 + P]) for p in range(2)]
        v_aug = [sb(f"v_aug{p}", [P, M_HEADS, M_DIM + 1]) for p in range(2)]
        o_th = [sb(f"o_th{p}", [P, M_WIDTH]) for p in range(2)]
        qg = [sb(f"qg{p}", [P, 2, P]) for p in range(2)]
        kg = [sb(f"kg{p}", [P, 2, P]) for p in range(2)]
        vg = [sb(f"vg{p}", [P, G_WIDTH]) for p in range(2)]
        gate2 = [sb(f"gate2{p}", [P, G_WIDTH]) for p in range(2)]
        misc = [sb(f"misc{p}", [P, MISC]) for p in range(2)]
        acc = sb("conv_acc", [P, KT, P])
        cth = sb("conv_tanh", [P, KT, P])
        qkT = sb("qkT", [P, KT, P])
        codeT = sb("codeT", [G_RANK, P])
        rows = {n: sb("row_" + n, [M_HEADS, P]) for n in
                ("fg", "ig", "ig2", "l", "lf", "b", "c", "a", "winter", "floor", "wk")}
        m_row = [sb(f"m_row{p}", [M_HEADS, P]) for p in range(2)]
        cols = sb("cols", [P, 3 * M_HEADS])
        dec = sb("dec", [P, M_HEADS])
        em = sb("em", [P, M_HEADS, P])
        pT = sb("pT", [P, M_HEADS, P])
        qs = sb("qs", [P, M_HEADS, P])
        kw = sb("kw", [P, M_HEADS, P])
        c_st = sb("c_state", [P, M_HEADS, M_DIM + 1])
        r4 = sb("r4", [P, M_HEADS])
        ri4 = sb("ri4", [P, M_HEADS])
        gx = sb("gx", [P, 2, P])
        gl = sb("gl", [P, 2, P])
        gb = sb("gb", [P, 2, P])
        bend = sb("bend", [P, 2])
        eb = sb("eb", [P, 2, P])
        ebe = sb("ebe", [P, 2, P])
        qi = sb("qi", [P, 2, P])
        ki = sb("ki", [P, 2, P])
        xl = sb("xl", [P, len(LEVELS), 2, P])
        khat = sb("khat", [P, 2 * P])
        aT = sb("aT", [P, G_HEADS, P])
        s_st = sb("s_state", [P, 2, G_V])
        sq = qs[:, :, :].rearrange("p a b -> p (a b)")
        ss8 = sb("ss8", [P, M_HEADS + G_HEADS])
        ms8 = sb("ms8", [P, M_HEADS + G_HEADS])
        rs8 = sb("rs8", [P, M_HEADS + G_HEADS])
        cmask = sb("cmask", [P, P])
        lmask = sb("lmask", [P, len(LEVELS) + 1, P], U8)
        sel = sb("sel", [M_HEADS, M_HEADS, P])
        ones_gk = sb("ones_gk", [P, P])
        y = acc[:, :, :].rearrange("p a b -> p (a b)")
        yT = cth
        lmask_f = em[:, 0, :]
        vrows = em[0:R_ALL, 1, :]
        bank = [ctx.enter_context(nc.psum_tensor(f"bank{i}", [P, 512], F32)) for i in range(8)]

        w_loaded = [sem(f"w_loaded{i}") for i in range(8)]
        vec_loaded, small_loaded = sem("vec_loaded"), sem("small_loaded")
        vec_T, vec_ready = sem("vec_T"), sem("vec_ready")
        consts, consts_v, x_zeroed = sem("consts"), sem("consts_v"), sem("x_zeroed")
        x_loaded, x_ss, x_rs, xn_ready = sem("x_loaded"), sem("x_ss"), sem("x_rs"), sem("xn_ready")
        xT_ready, xnT_ready = sem("xT_ready"), sem("xnT_ready")
        q_ready, q_out, k_ready, k_out = sem("q_ready"), sem("q_out"), sem("k_ready"), sem("k_out")
        qkg_ready, qkg_out = sem("qkg_ready"), sem("qkg_out")
        v_ready, v_out, o_ready, o_out = sem("v_ready"), sem("v_out"), sem("o_ready"), sem("o_out")
        vg_ready, vg_out = sem("vg_ready"), sem("vg_out")
        gg_ready, gg_tanh, gate_done = sem("gg_ready"), sem("gg_tanh"), sem("gate_done")
        misc_ready, misc_out = sem("misc_ready"), sem("misc_out")
        gT_ready, gates_x, codeT_out = sem("gT_ready"), sem("gates_x"), sem("codeT_out")
        la_ready, gx_ready = sem("la_ready"), sem("gx_ready")
        ln_m, ln_g = sem("ln_m"), sem("ln_g")
        rows_ready, rows_exp = sem("rows_ready"), sem("rows_exp")
        conv_done, conv_tanh, qkT_ready = sem("conv_done"), sem("conv_tanh_s"), sem("qkT_ready")
        gb_ready, eb_ready, diff_ready, ediff_ready = sem("gb_ready"), sem("eb_ready"), sem("diff_ready"), sem("ediff_ready")
        qi_ready, kgt_ready, khat_out = sem("qi_ready"), sem("kgt_ready"), sem("khat_out")
        bc_ready, cols_ready, em_in, qs_ready, em_exp = (sem("bc_ready"), sem("cols_ready"), sem("em_in"),
                                                         sem("qs_ready"), sem("em_exp"))
        st_ready, pT_ready, kT_ready, kw_ready = sem("st_ready"), sem("pT_ready"), sem("kT_ready"), sem("kw_ready")
        xl_ready, lvl_ready, lvl_done = sem("xl_ready"), sem("lvl_ready"), sem("lvl_done")
        num_ready, h_ready, cu_ready, c_done = sem("num_ready"), sem("h_ready"), sem("cu_ready"), sem("c_done")
        og_ready, su_ready, s_done = sem("og_ready"), sem("su_ready"), sem("s_done")
        sqm_ready, sqg_ready, ss_ready, rs_ready = sem("sqm_ready"), sem("sqg_ready"), sem("ss_ready"), sem("rs_ready")
        og_used, y_ready, yT_ready, yT_out, yT_stored = (sem("og_used"), sem("y_ready"), sem("yT_ready"),
                                                         sem("yT_out"), sem("yT_stored"))
        act_seq, dve_seq, pool_seq = sem("act_seq"), sem("dve_seq"), sem("pool_seq")
        w_out_loaded = [sem(f"w_out_loaded{g}") for g in range(2)]
        w_out_hi, w_out_lo = sem("w_out_hi"), sem("w_out_lo")

        block = ctx.enter_context(nc.Block())
        N_LOOP = (CHUNKS - 3) // 2

        def chunk_program(eng, mix, before_last=None):
            mix(0, 0)
            with eng.Fori(0, N_LOOP) as j:
                for p in range(2):
                    mix(j * 2 + (1 + p), 1 - p)
            mix(CHUNKS - 2, (CHUNKS - 2) % 2)
            if before_last:
                before_last()
            mix(CHUNKS - 1, (CHUNKS - 1) % 2)

        def is_last(c):
            return isinstance(c, int) and c == CHUNKS - 1

        W_PARTS = [(C_QK, C_QK + M_WIDTH), (C_QK + M_WIDTH, C_V), (C_QG, C_VG), (C_V, C_O), (C_O, C_GATES),
                   (C_VG, C_GG), (C_GG, C_CODE)]

        @block.sync
        def _(sp):
            sp.wait_ge(x_zeroed, 1)
            sp.dma_start(x_in[PAD:P, :], t["meta_tokens"]).then_inc(x_loaded, 16)
            n = 0
            for src, row in ((t["norm1_g"], R_NORM1), (t["conv_w"], R_CONVW), (t["conv_b"], R_CONVB),
                             (t["a_b"], R_AB), (t["m_norm_g"], R_MG), (t["g_norm_g"], R_GG)):
                count = src.shape[0] * src.shape[1] // P
                sp.dma_start(vrows[row:row + count, :], src.rearrange("a (k p) -> (a k) p", p=P)).then_inc(vec_loaded, 16)
                n += 1
            sp.dma_start(gate_bi[:, :], t["gate_b"][0:1, :].rearrange("o h -> h o")).then_inc(small_loaded, 16)
            sp.dma_start(gate_bf[:, :], t["gate_b"][1:2, :].rearrange("o h -> h o")).then_inc(small_loaded, 16)
            sp.dma_start(a_w2[:, :], t["a_w2"]).then_inc(small_loaded, 16)
            w_rows = t["w_in"].rearrange("(k p) n -> p k n", p=P)
            for i, (lo, hi) in enumerate(W_PARTS):
                sp.dma_start(w_in[:, :, lo:hi], w_rows[:, :, lo:hi]).then_inc(w_loaded[i], 16)
            sp.dma_start(w_in[:, :, C_GATES:C_QG], w_rows[:, :, C_GATES:C_QG]).then_inc(w_loaded[7], 16)
            sp.dma_start(w_in[:, :, C_CODE:IN_WIDTH], w_rows[:, :, C_CODE:IN_WIDTH]).then_inc(w_loaded[7], 16)
            sp.wait_ge(xn_ready, 1)
            sp.dma_start(x_in[:, :], at(t["x"], 0)).then_inc(x_loaded, 16)

            def mix(c, par):
                if not (isinstance(c, int) and c + 2 >= CHUNKS):
                    sp.wait_ge(xn_ready, c + 2)
                    sp.dma_start(x_in[:, :], at(t["x"], c + 1)).then_inc(x_loaded, 16)
                sp.wait_ge(yT_out, c + 1)
                sp.dma_start(at(t["yT"], c), yT[:, :, :].rearrange("p a b -> p (a b)")).then_inc(yT_stored, 16)

            def before_last():
                sp.wait_ge(misc_ready, CHUNKS)
                w_out = t["w_out"].rearrange("(k p) n -> p k n", p=P)
                raw = views["w_raw"].rearrange("p (k n) -> p k n", k=KT)
                for g in range(2):
                    ks = slice(g * KT // 2, (g + 1) * KT // 2)
                    sp.dma_start(raw[:, ks, :], w_out[:, ks, :]).then_inc(w_out_loaded[g], 16)
                for p in range(2):
                    sp.dma_start(views[f"yT_{p}"], at(t["yT"], 1 + p)).then_inc(c_all["y_loaded"][p], 16)
                    sp.dma_start(views[f"h_{p}"], at(t["x"], p)).then_inc(c_all["x_loaded"][p], 16)

            chunk_program(sp, mix, before_last)
            sp.wait_ge(yT_stored, 16 * CHUNKS)

        @block.gpsimd
        def _(pool):
            n = [0]

            def link(ins):
                n[0] += 1
                ins.then_inc(pool_seq, 1)
                pool.wait_ge(pool_seq, n[0])

            pool.memset(x_in[:, :], 0.0).then_inc(x_zeroed, 1)
            link(pool.memset(ident[:, :], 0.0))
            link(pool.affine_select(out=ident[:, :], in_=ident[:, :], compare_op=ALU.not_equal, fill=1.0, base=0,
                                    pattern=[[-1, P]], channel_multiplier=1))
            link(pool.memset(xn[:, :], 0.0))
            link(pool.memset(mhalf[:, :], -0.5))
            link(pool.memset(eps_col[:, :], EPS))
            link(pool.memset(cmask[:, :], 0.0))
            link(pool.affine_select(out=cmask[:, :], in_=cmask[:, :], compare_op=ALU.is_ge, fill=NEG, base=0,
                                    pattern=[[1, P]], channel_multiplier=-1))
            for i, half in enumerate(LEVELS):
                size = 2 * half
                m = lmask_f.rearrange("p (b h r) -> p b h r", h=2, r=half)
                link(pool.memset(lmask_f, 0.0))
                link(pool.memset(m[:, :, 1, :], 1.0))
                link(pool.affine_select(out=lmask_f.rearrange("p (b r) -> p b r", r=size),
                                        in_=lmask_f.rearrange("p (b r) -> p b r", r=size), compare_op=ALU.is_ge,
                                        fill=0.0, base=0, pattern=[[-size, P // size], [0, size]], channel_multiplier=1))
                link(pool.affine_select(out=lmask_f.rearrange("p (b r) -> p b r", r=size),
                                        in_=lmask_f.rearrange("p (b r) -> p b r", r=size), compare_op=ALU.is_ge,
                                        fill=0.0, base=half - 1, pattern=[[size, P // size], [0, size]],
                                        channel_multiplier=-1))
                link(pool.tensor_copy(lmask[:, i, :], lmask_f))
            link(pool.tensor_copy(lmask[:, len(LEVELS), :], ident[:, :]))
            for h in range(M_HEADS):
                link(pool.tensor_copy(sel[:, h, :], ident[0:M_HEADS, h:h + 1].to_broadcast([M_HEADS, P])))
            pool.memset(aT[:, :, :], 0.0).then_inc(consts, 1)

            def x_power(m):
                pool.wait_ge(x_ss, m + 1)
                pool.tensor_tensor(xms[:, :], xss[:, :], eps_col[:, :], ALU.add).then_inc(pool_seq, 1)
                n[0] += 1
                pool.wait_ge(pool_seq, n[0])
                pool.tensor_tensor(xrs[:, :], xms[:, :], mhalf[:, 0:1], ALU.pow).then_inc(x_rs, 1)

            x_power(0)
            x_power(1)

            def mix(c, par):
                if not (isinstance(c, int) and c + 2 >= CHUNKS):
                    x_power(c + 2)
                pool.wait_ge(ss_ready, c + 1)
                pool.tensor_tensor(rs8[:, :], ms8[:, :], mhalf[:, :], ALU.pow).then_inc(rs_ready, 1)
                pool.sem_clear(pool_seq)
                n[0] = 0

            pool.sem_clear(pool_seq)
            n[0] = 0

            def before_last():
                for k in range(KT):
                    at_k = slice(k * D_MODEL, (k + 1) * D_MODEL)
                    pool.wait_ge(w_out_hi, k + 1)
                    pool.tensor_tensor(views["w_lo"][:, at_k], views["w_raw"][:, at_k],
                                       views["w_hi"][:, at_k].bitcast(F32), ALU.subtract).then_inc(w_out_lo, 1)
                pool.wait_ge(w_out_lo, KT)
                pool.sem_clear(w_out_lo)
                pool.sem_clear(w_out_hi)

            chunk_program(pool, mix, before_last)

        @block.scalar
        def _(act):
            n = [0]

            def link(ins):
                n[0] += 1
                ins.then_inc(act_seq, 1)
                act.wait_ge(act_seq, n[0])

            def x_norm(m):
                act.wait_ge(x_loaded, 16 * (m + 1))
                if not isinstance(m, int) or m > 0:
                    act.wait_ge(xT_ready, m)
                nc.scalar.activation(xn[:, :], x_in[:, :], ACT.Square, scale=D_MODEL ** -0.5,
                                     accum_out=xss[:, :]).then_inc(x_ss, 1)
                act.wait_ge(x_rs, m + 1)
                act.wait_ge(x_ss, m + 1)
                nc.scalar.activation(xn[:, :], x_in[:, :], ACT.Copy, scale=xrs[:, :]).then_inc(xn_ready, 1)

            def out_q(m, par):
                act.wait_ge(q_ready, m + 1)
                nc.scalar.activation(conv_in[par][:, 0:4, CONV_K - 1:], bank[0][:, :].rearrange("p (a b) -> p a b", a=4),
                                     ACT.Copy).then_inc(q_out, 1)

            def out_k(m, par):
                act.wait_ge(k_ready, m + 1)
                nc.scalar.activation(conv_in[par][:, 4:8, CONV_K - 1:], bank[1][:, :].rearrange("p (a b) -> p a b", a=4),
                                     ACT.Copy).then_inc(k_out, 1)

            def out_qkg(m, par):
                act.wait_ge(qkg_ready, m + 1)
                b = bank[0][:, :].rearrange("p (a b) -> p a b", a=4)
                nc.scalar.activation(qg[par][:, :, :], b[:, 0:2, :], ACT.Copy, scale=G_K ** -0.5).then_inc(act_seq, 1)
                n[0] += 1
                nc.scalar.activation(kg[par][:, :, :], b[:, 2:4, :], ACT.Copy).then_inc(qkg_out, 1)

            def out_v(m, par):
                act.wait_ge(v_ready, m + 1)
                nc.scalar.activation(v_aug[par][:, :, 0:M_DIM], bank[1][:, :].rearrange("p (a b) -> p a b", a=4),
                                     ACT.Copy).then_inc(v_out, 1)

            def out_o(m, par):
                act.wait_ge(o_ready, m + 1)
                nc.scalar.activation(o_th[par][:, :], bank[0][:, :], ACT.Tanh, scale=0.5).then_inc(o_out, 1)

            def out_vg(m, par):
                act.wait_ge(vg_ready, m + 1)
                nc.scalar.activation(vg[par][:, :], bank[1][:, :], ACT.Copy).then_inc(vg_out, 1)

            def out_gg(m, par):
                act.wait_ge(gg_ready, m + 1)
                nc.scalar.activation(gate2[par][:, :], bank[0][:, :], ACT.Tanh, scale=0.5).then_inc(gg_tanh, 1)

            def out_misc(m, par):
                act.wait_ge(misc_ready, m + 1)
                nc.scalar.activation(misc[par][:, :], bank[4][:, 0:MISC], ACT.Copy).then_inc(misc_out, 1)

            act.wait_ge(consts, 1)
            x_norm(0)
            for f in (out_q, out_k, out_qkg, out_v, out_o, out_vg, out_gg, out_misc):
                f(0, 0)
            x_norm(1)

            def mix(c, par):
                last, nxt = is_last(c), 1 - par
                act.wait_ge(gates_x, c + 1)
                link(nc.scalar.activation(rows["l"][:, :], rows["fg"][:, :], ACT.Abs))
                link(nc.scalar.activation(rows["l"][:, :], rows["l"][:, :], ACT.Exp, scale=-1.0))
                act.wait_ge(gx_ready, c + 1)
                link(nc.scalar.activation(gl[:, :, :], gx[:, :, :], ACT.Abs))
                link(nc.scalar.activation(gl[:, :, :], gl[:, :, :], ACT.Exp, scale=-1.0))
                nc.scalar.activation(rows["l"][:, :], rows["l"][:, :], ACT.Ln, bias=1.0).then_inc(ln_m, 1)
                nc.scalar.activation(gl[:, :, :], gl[:, :, :], ACT.Ln, bias=1.0).then_inc(ln_g, 1)
                act.wait_ge(rows_ready, c + 1)
                link(nc.scalar.activation(rows["winter"][:, :], rows["c"][:, :], ACT.Exp, bias=m_row[nxt][:, P - 1:P]))
                link(nc.scalar.activation(rows["floor"][:, :], m_row[par][:, :], ACT.Exp, scale=-1.0))
                nc.scalar.activation(rows["wk"][:, :], rows["a"][:, :], ACT.Exp,
                                     bias=rows["c"][:, P - 1:P]).then_inc(rows_exp, 1)
                act.wait_ge(gb_ready, c + 1)
                link(nc.scalar.activation(eb[:, :, :], gb[:, :, :], ACT.Exp, scale=1 / G_TAU))
                for j in range(2):
                    e = nc.scalar.activation(ebe[:, j, :], gb[:, j, :], ACT.Exp, scale=-1 / G_TAU, bias=bend[:, j:j + 1])
                    if j == 0:
                        link(e)
                e.then_inc(eb_ready, 1)
                act.wait_ge(diff_ready, c + 1)
                link(nc.scalar.activation(xl[:, :, :, :], xl[:, :, :, :], ACT.Abs))
                nc.scalar.activation(xl[:, :, :, :], xl[:, :, :, :], ACT.Exp, scale=-1 / G_TAU).then_inc(ediff_ready, 1)
                act.wait_ge(conv_done, c + 1)
                if not isinstance(c, int) or c > 0:
                    act.wait_ge(yT_stored, 16 * c)
                nc.scalar.activation(cth[:, :, :], acc[:, :, :], ACT.Tanh, scale=0.5).then_inc(conv_tanh, 1)
                if not last:
                    link(nc.scalar.activation(conv_in[nxt][:, :, 0:CONV_K - 1], conv_in[par][:, :, P:], ACT.Copy))
                    out_q(c + 1, nxt)
                    out_k(c + 1, nxt)
                act.wait_ge(em_in, c + 1)
                act.wait_ge(cols_ready, c + 1)
                for h in range(M_HEADS):
                    e = nc.scalar.activation(em[:, h, :], em[:, h, :], ACT.Exp, bias=cols[:, h:h + 1])
                    if h < M_HEADS - 1:
                        link(e)
                e.then_inc(em_exp, 1)
                act.wait_ge(kgt_ready, c + 1)
                nc.scalar.activation(khat[:, :], bank[5][:, 0:2 * P], ACT.Copy).then_inc(khat_out, 1)
                if last:
                    for k in range(KT):
                        if k % (KT // 2) == 0:
                            act.wait_ge(w_out_loaded[k // (KT // 2)], 16)
                        w_k = views["w_raw"][:, k * D_MODEL:(k + 1) * D_MODEL]
                        link(nc.scalar.activation(w_k, w_k, ACT.Copy, scale=vec[:, R_MG + k:R_MG + k + 1]))
                        nc.scalar.activation(views["w_hi"][:, k * D_MODEL:(k + 1) * D_MODEL], w_k,
                                             ACT.Copy).then_inc(w_out_hi, 1)
                    for g in range(2):
                        act.sem_clear(w_out_loaded[g])
                if not last:
                    out_qkg(c + 1, nxt)
                    if not (isinstance(c, int) and c + 2 >= CHUNKS):
                        x_norm(c + 2)
                    out_v(c + 1, nxt)
                act.wait_ge(h_ready, c + 1)
                nc.scalar.activation(sq, y[:, 0:M_WIDTH], ACT.Square).then_inc(sqm_ready, 1)
                if not last:
                    out_o(c + 1, nxt)
                act.wait_ge(og_ready, c + 1)
                for odd in range(2):
                    e = nc.scalar.activation(em[:, odd::2, :], bank[6 + odd][:, 0:2 * P].rearrange("p (a b) -> p a b", a=2),
                                             ACT.Square)
                    if odd == 0:
                        link(e)
                e.then_inc(sqg_ready, 1)
                if not last:
                    out_vg(c + 1, nxt)
                    out_gg(c + 1, nxt)
                    out_misc(c + 1, nxt)
                act.wait_ge(yT_ready, c + 1)
                for half in range(2):
                    e = nc.scalar.activation(yT[:, 4 * half:4 * half + 4, :],
                                             bank[2 + half][:, :].rearrange("p (a b) -> p a b", a=4), ACT.Copy)
                    if half == 0:
                        link(e)
                e.then_inc(yT_out, 1)
                act.wait_ge(act_seq, n[0])
                act.sem_clear(act_seq)
                n[0] = 0

            act.wait_ge(act_seq, n[0])
            act.sem_clear(act_seq)
            n[0] = 0
            chunk_program(act, mix)

        @block.tensor
        def _(pe):
            def channels(dst, col, tiles):
                for i in range(tiles):
                    for k in range(KT):
                        mm = nc.tensor.matmul(dst[:, i * P:(i + 1) * P], w_in[:, k, col + i * P:col + (i + 1) * P],
                                              xnT[:, k, :], start=(k == 0), stop=(k == KT - 1))
                return mm

            def tokens(dst, col, width):
                for k in range(KT):
                    mm = nc.tensor.matmul(dst, xnT[:, k, :], w_in[:, k, col:col + width],
                                          start=(k == 0), stop=(k == KT - 1))
                return mm

            def x_T(m):
                pe.wait_ge(xn_ready, m + 1)
                for k in range(KT):
                    b = bank[2 + k // 4]
                    mm = nc.tensor.transpose(b[:, (k % 4) * P:(k % 4 + 1) * P], xn[:, k * P:(k + 1) * P], ident[:, :])
                mm.then_inc(xT_ready, 1)

            def first(m, i):
                if isinstance(m, int) and m == 0:
                    pe.wait_ge(w_loaded[i], 16 if i < 7 else 32)

            def p_q(m):
                first(m, 0)
                pe.wait_ge(xnT_ready, m + 1)
                wait(pe, gate_done, m)
                channels(bank[0], C_QK, 4).then_inc(q_ready, 1)

            def p_k(m):
                first(m, 1)
                wait(pe, vg_out, m)
                channels(bank[1], C_QK + M_WIDTH, 4).then_inc(k_ready, 1)

            def p_qkg(m):
                first(m, 2)
                pe.wait_ge(q_out, m + 1)
                channels(bank[0], C_QG, 4).then_inc(qkg_ready, 1)

            def p_v(m):
                first(m, 3)
                pe.wait_ge(k_out, m + 1)
                tokens(bank[1][:, :], C_V, M_WIDTH).then_inc(v_ready, 1)

            def p_o(m):
                first(m, 4)
                pe.wait_ge(qkg_out, m + 1)
                tokens(bank[0][:, :], C_O, M_WIDTH).then_inc(o_ready, 1)

            def p_vg(m):
                first(m, 5)
                pe.wait_ge(v_out, m + 1)
                tokens(bank[1][:, :], C_VG, G_WIDTH).then_inc(vg_ready, 1)

            def p_gg(m):
                first(m, 6)
                pe.wait_ge(o_out, m + 1)
                tokens(bank[0][:, :], C_GG, G_WIDTH).then_inc(gg_ready, 1)

            def p_misc(m):
                first(m, 7)
                wait(pe, c_done, m)
                tokens(bank[4][:, 0:2 * M_HEADS], C_GATES, 2 * M_HEADS)
                tokens(bank[4][:, 2 * M_HEADS:MISC], C_CODE, G_RANK).then_inc(misc_ready, 1)

            pe.wait_ge(consts, 1)
            pe.wait_ge(vec_loaded, 16 * 6)
            nc.tensor.transpose(bank[7][:, 0:R_ALL], vrows, ident[0:R_ALL, 0:R_ALL]).then_inc(vec_T, 1)
            x_T(0)
            for f in (p_q, p_k, p_qkg, p_v, p_o, p_vg, p_gg, p_misc):
                f(0)
            pe.wait_ge(small_loaded, 48)
            pe.wait_ge(consts_v, 1)

            def mix(c, par):
                last = is_last(c)
                pe.wait_ge(misc_out, c + 1)
                nc.tensor.transpose(bank[4][0:M_HEADS, 0:P], misc[par][:, 0:M_HEADS], ident[:, :])
                nc.tensor.transpose(bank[4][0:M_HEADS, P:2 * P], misc[par][:, M_HEADS:2 * M_HEADS], ident[:, :])
                nc.tensor.transpose(bank[4][0:G_RANK, 2 * P:3 * P], misc[par][:, 2 * M_HEADS:], ident[:, :]).then_inc(gT_ready, 1)
                if not last:
                    wait(pe, yT_out, c)
                    x_T(c + 1)
                pe.wait_ge(codeT_out, c + 1)
                wait(pe, h_ready, c)
                for j in range(2):
                    mm = nc.tensor.matmul(bank[5][:, j * P:(j + 1) * P], a_w2[:, j * P:(j + 1) * P], codeT[:, :],
                                          start=True, stop=True)
                mm.then_inc(la_ready, 1)
                if not last:
                    p_q(c + 1)
                    p_k(c + 1)
                pe.wait_ge(rows_exp, c + 1)
                pe.wait_ge(gx_ready, c + 1)
                wait(pe, og_used, c)
                for h in range(M_HEADS):
                    nc.tensor.matmul(bank[6][:, h * P:(h + 1) * P], sel[:, h, :], rows["c"][:, :], start=True, stop=True)
                for h in range(M_HEADS):
                    nc.tensor.matmul(bank[7][:, h * P:(h + 1) * P], sel[:, h, :], rows["winter"][:, :], start=True, stop=True)
                for i, r in enumerate(("a", "floor", "wk")):
                    mm = nc.tensor.transpose(bank[5][:, 2 * P + 4 * i:2 * P + 4 * i + 4], rows[r][:, :],
                                             ident[0:M_HEADS, 0:M_HEADS])
                mm.then_inc(bc_ready, 1)
                pe.wait_ge(qkT_ready, c + 1)
                for h in range(M_HEADS):
                    mm = nc.tensor.matmul(bank[4][:, h * P:(h + 1) * P], qkT[:, M_HEADS + h, :], qkT[:, h, :],
                                          start=True, stop=True)
                mm.then_inc(st_ready, 1)
                if not last:
                    pe.wait_ge(xnT_ready, c + 2)
                else:
                    pe.wait_ge(yT_out, c)
                for h in range(M_HEADS):
                    mm = nc.tensor.transpose(bank[2][:, h * P:(h + 1) * P], qkT[:, M_HEADS + h, :], ident[:, :])
                mm.then_inc(kT_ready, 1)
                pe.wait_ge(qi_ready, c + 1)
                pe.wait_ge(cols_ready, c + 1)
                for j in range(2):
                    mm = nc.tensor.transpose(bank[5][:, j * P:(j + 1) * P], ki[:, j, :], ident[:, :])
                mm.then_inc(kgt_ready, 1)
                if not last:
                    p_qkg(c + 1)
                pe.wait_ge(xl_ready, c + 1)
                pe.wait_ge(em_in, c + 1)
                pe.wait_ge(qs_ready, c + 1)
                pe.wait_ge(khat_out, c + 1)
                for i in range(len(LEVELS) + 1):
                    pair, half = LEVEL_BANKS[i // 2 % 2], i % 2
                    if i // 2 >= 2 and half == 0:
                        pe.wait_ge(lvl_done, i // 2 - 1)
                    for h in range(G_HEADS):
                        part = slice(G_K * (h % 2), G_K * (h % 2) + G_K)
                        if i < len(LEVELS):
                            k_side = q_side = xl[part, i, h // 2, :]
                        else:
                            k_side, q_side = kg[par][part, h // 2, :], qg[par][part, h // 2, :]
                        col = (2 * half + h // 2) * P
                        mm = nc.tensor.matmul(bank[pair[h % 2]][:, col:col + P], k_side, q_side, start=True, stop=True)
                    if half == 1:
                        mm.then_inc(lvl_ready, 1)
                    if i == 3 and not last:
                        p_v(c + 1)
                pe.wait_ge(lvl_done, (len(LEVELS) + 1) // 2)
                pe.sem_clear(lvl_done)
                pe.wait_ge(pT_ready, c + 1)
                wait(pe, c_done, c)
                for h in range(M_HEADS):
                    dst = bank[3 + 2 * (h // 2)][:, (h % 2) * 256:(h % 2) * 256 + M_DIM + 1]
                    nc.tensor.matmul(dst, pT[:, h, :], v_aug[par][:, h, :], start=True, stop=False)
                    mm = nc.tensor.matmul(dst, qs[:, h, :], c_st[:, h, :], start=False, stop=True)
                mm.then_inc(num_ready, 1)
                pe.wait_ge(kw_ready, c + 1)
                for h in range(M_HEADS):
                    dst = bank[4 - 2 * (h // 2)][:, (h % 2) * 256:(h % 2) * 256 + M_DIM + 1]
                    mm = nc.tensor.matmul(dst, kw[:, h, :], v_aug[par][:, h, :], start=True, stop=True)
                mm.then_inc(cu_ready, 1)
                if not last:
                    p_o(c + 1)
                wait(pe, s_done, c)
                for h in range(G_HEADS):
                    part = slice(G_K * (h % 2), G_K * (h % 2) + G_K)
                    dst = bank[6 + h % 2][:, (h // 2) * P:(h // 2 + 1) * P]
                    nc.tensor.matmul(dst, aT[:, h, :], vg[par][:, h * P:(h + 1) * P], start=True, stop=False)
                    mm = nc.tensor.matmul(dst, qi[part, h // 2, :], s_st[part, h // 2, :], start=False, stop=True)
                mm.then_inc(og_ready, 1)
                pe.wait_ge(h_ready, c + 1)
                for j in range(2):
                    mm = nc.tensor.matmul(bank[3][:, j * 2 * P:(j + 1) * 2 * P], khat[:, j * P:(j + 1) * P],
                                          vg[par][:, j * 2 * P:(j + 1) * 2 * P], start=True, stop=True)
                mm.then_inc(su_ready, 1)
                if not last:
                    p_vg(c + 1)
                    p_gg(c + 1)
                    p_misc(c + 1)
                pe.wait_ge(y_ready, c + 1)
                pe.wait_ge(c_done, c + 1)
                pe.wait_ge(s_done, c + 1)
                for k in range(KT):
                    mm = nc.tensor.transpose(bank[2 + k // 4][:, (k % 4) * P:(k % 4 + 1) * P], y[:, k * P:(k + 1) * P],
                                             ident[:, :])
                mm.then_inc(yT_ready, 1)

            chunk_program(pe, mix)

        @block.vector
        def _(v):
            n = [0]

            def step(ins):
                n[0] += 1
                ins.then_inc(dve_seq, 1)

            def settle():
                v.wait_ge(dve_seq, n[0])

            def link(ins):
                step(ins)
                settle()

            v.wait_ge(vec_T, 1)
            nc.vector.tensor_copy(vec[:, :], bank[7][:, 0:R_ALL]).then_inc(vec_ready, 1)
            v.wait_ge(vec_ready, 1)
            step(nc.vector.memset(c_st[:, :, :], 0.0))
            step(nc.vector.memset(s_st[:, :, :], 0.0))
            step(nc.vector.memset(m_row[1][:, :], 0.0))
            step(nc.vector.memset(ones_gk[:, :], 1.0))
            step(nc.vector.memset(conv_in[0][:, :, 0:CONV_K - 1], 0.0))
            for p in range(2):
                step(nc.vector.memset(v_aug[p][:, :, M_DIM:M_DIM + 1], 1.0))
            settle()
            nc.vector.memset(bend[:, :], 0.0).then_inc(consts_v, 1)
            v.wait_ge(consts_v, 1)
            v.wait_ge(small_loaded, 48)

            def out_xT(m):
                v.wait_ge(xT_ready, m + 1)
                wait(v, misc_ready, m)
                for half in range(2):
                    g = vec[:, R_NORM1 + 4 * half:R_NORM1 + 4 * half + 4]
                    e = nc.vector.tensor_tensor(xnT[:, 4 * half:4 * half + 4, :],
                                                bank[2 + half][:, :].rearrange("p (a b) -> p a b", a=4),
                                                g.unsqueeze(2).to_broadcast([P, 4, P]), ALU.mult)
                    if half == 0:
                        step(e)
                e.then_inc(xnT_ready, 1)

            def out_gate(m, par):
                v.wait_ge(gg_tanh, m + 1)
                nc.vector.scalar_tensor_tensor(gate2[par][:, :], gate2[par][:, :], 1.0, bank[0][:, :],
                                               ALU.add, ALU.mult).then_inc(gate_done, 1)

            out_xT(0)
            out_gate(0, 0)

            def mix(c, par):
                last, nxt = is_last(c), 1 - par
                head0 = isinstance(c, int) and c == 0
                v.wait_ge(gT_ready, c + 1)
                nc.vector.tensor_copy(codeT[:, :], bank[4][0:G_RANK, 2 * P:3 * P]).then_inc(codeT_out, 1)
                step(nc.vector.tensor_scalar(rows["ig"][:, :], bank[4][0:M_HEADS, 0:P], gate_bi[:, :], None, ALU.add))
                step(nc.vector.tensor_scalar(rows["ig2"][:, :], bank[4][0:M_HEADS, 0:P], gate_bi[:, :], LN_QK,
                                             ALU.add, ALU.add))
                if head0:
                    settle()
                    step(nc.vector.memset(rows["ig"][:, 0:PAD], NEG))
                    step(nc.vector.memset(rows["ig2"][:, 0:PAD], NEG))
                nc.vector.tensor_scalar(rows["fg"][:, :], bank[4][0:M_HEADS, P:2 * P], gate_bf[:, :], None,
                                        ALU.add).then_inc(gates_x, 1)
                if not last:
                    out_xT(c + 1)
                v.wait_ge(la_ready, c + 1)
                for j in range(2):
                    e = nc.vector.tensor_scalar(gx[:, j, :], bank[5][:, j * P:(j + 1) * P],
                                                vec[:, R_AB + j:R_AB + j + 1], None, ALU.add)
                    if j == 0:
                        step(e)
                e.then_inc(gx_ready, 1)
                v.wait_ge(k_out, c + 1)
                wait(v, yT_ready, c)
                for j in range(CONV_K):
                    for i in range(KT):
                        w = vec[:, R_CONVW + j * KT + i:R_CONVW + j * KT + i + 1]
                        src = conv_in[par][:, i, j:j + P]
                        if j == 0:
                            e = nc.vector.tensor_scalar(acc[:, i, :], src, w, vec[:, R_CONVB + i:R_CONVB + i + 1],
                                                        ALU.mult, ALU.add)
                        else:
                            e = nc.vector.scalar_tensor_tensor(acc[:, i, :], src, w, acc[:, i, :], ALU.mult, ALU.add)
                        if (j, i) != (CONV_K - 1, KT - 1):
                            step(e)
                    if j < CONV_K - 1:
                        settle()
                e.then_inc(conv_done, 1)
                v.wait_ge(ln_m, c + 1)
                link(nc.vector.scalar_tensor_tensor(rows["lf"][:, :], rows["fg"][:, :], 0.0, rows["l"][:, :],
                                                    ALU.min, ALU.subtract))
                if head0:
                    link(nc.vector.memset(rows["lf"][:, 0:PAD], 0.0))
                step(nc.vector.tensor_tensor_scan(rows["b"][:, :], ones_gk[0:M_HEADS, :], rows["lf"][:, :], 0.0,
                                                  ALU.mult, ALU.add))
                link(nc.vector.tensor_tensor_scan(m_row[par][:, :], rows["lf"][:, :], rows["ig"][:, :],
                                                  m_row[nxt][:, P - 1:P], ALU.add, ALU.max))
                step(nc.vector.tensor_tensor(rows["a"][:, :], rows["ig2"][:, :], rows["b"][:, :], ALU.subtract))
                nc.vector.tensor_tensor(rows["c"][:, :], rows["b"][:, :], m_row[par][:, :],
                                        ALU.subtract).then_inc(rows_ready, 1)
                v.wait_ge(ln_g, c + 1)
                link(nc.vector.scalar_tensor_tensor(gx[:, :, :], gx[:, :, :], 0.0, gl[:, :, :], ALU.min, ALU.subtract))
                for j in range(2):
                    step(nc.vector.tensor_tensor_scan(gb[:, j, :], ones_gk[:, :], gx[:, j, :], 0.0, ALU.mult, ALU.add))
                settle()
                nc.vector.tensor_scalar(bend[:, :], gb[:, :, P - 1], 1 / G_TAU, None, ALU.mult).then_inc(gb_ready, 1)
                for i, half in enumerate(LEVELS):
                    size = 2 * half
                    g = gb[:, :, :].rearrange("p j (b r) -> p j b r", r=size)
                    e = nc.vector.tensor_tensor(xl[:, i, :, :].rearrange("p j (b r) -> p j b r", r=size), g,
                                                g[:, :, :, half - 1:half].to_broadcast([P, 2, P // size, size]),
                                                ALU.subtract)
                    if i < len(LEVELS) - 1:
                        step(e)
                e.then_inc(diff_ready, 1)
                v.wait_ge(conv_tanh, c + 1)
                nc.vector.scalar_tensor_tensor(qkT[:, :, :], cth[:, :, :], 1.0, acc[:, :, :],
                                               ALU.add, ALU.mult).then_inc(qkT_ready, 1)
                v.wait_ge(eb_ready, c + 1)
                step(nc.vector.tensor_tensor(ki[:, :, :], kg[par][:, :, :], ebe[:, :, :], ALU.mult))
                nc.vector.tensor_tensor(qi[:, :, :], qg[par][:, :, :], eb[:, :, :], ALU.mult).then_inc(qi_ready, 1)
                v.wait_ge(bc_ready, c + 1)
                nc.vector.tensor_copy(cols[:, :], bank[5][:, 2 * P:2 * P + 3 * M_HEADS]).then_inc(cols_ready, 1)
                nc.vector.tensor_tensor(em[:, :, :], bank[6][:, :].rearrange("p (a b) -> p a b", a=4),
                                        cmask[:, :].unsqueeze(1).to_broadcast([P, M_HEADS, P]), ALU.add).then_inc(em_in, 1)
                w4 = bank[7][:, :].rearrange("p (a b) -> p a b", a=4)
                step(nc.vector.tensor_copy(dec[:, :], w4[:, :, P - 1]))
                v.wait_ge(qkT_ready, c + 1)
                nc.vector.tensor_tensor(qs[:, :, :], w4, qkT[:, 0:M_HEADS, :], ALU.mult).then_inc(qs_ready, 1)
                v.wait_ge(kT_ready, c + 1)
                v.wait_ge(cols_ready, c + 1)
                nc.vector.tensor_tensor(kw[:, :, :], bank[2][:, :].rearrange("p (a b) -> p a b", a=4),
                                        cols[:, 2 * M_HEADS:].unsqueeze(2).to_broadcast([P, M_HEADS, P]),
                                        ALU.mult).then_inc(kw_ready, 1)
                v.wait_ge(ediff_ready, c + 1)
                for i, half in enumerate(LEVELS):
                    for side, src in ((0, kg), (1, qg)):
                        xv = xl[:, i, :, :].rearrange("p j (b h r) -> p j b h r", h=2, r=half)[:, :, :, side, :]
                        sv = src[par][:, :, :].rearrange("p j (b h r) -> p j b h r", h=2, r=half)[:, :, :, side, :]
                        e = nc.vector.tensor_tensor(xv, xv, sv, ALU.mult)
                        if (i, side) != (len(LEVELS) - 1, 1):
                            step(e)
                e.then_inc(xl_ready, 1)
                v.wait_ge(st_ready, c + 1)
                v.wait_ge(em_exp, c + 1)
                nc.vector.tensor_tensor(pT[:, :, :], bank[4][:, :].rearrange("p (a b) -> p a b", a=4), em[:, :, :],
                                        ALU.mult).then_inc(pT_ready, 1)
                for i in range(len(LEVELS) + 1):
                    pair, half = LEVEL_BANKS[i // 2 % 2], i % 2
                    if half == 0:
                        v.wait_ge(lvl_ready, i // 2 + 1)
                    settle()
                    for odd in range(2):
                        e = nc.vector.copy_predicated(
                            aT[:, odd::2, :], lmask[:, i, :].unsqueeze(1).to_broadcast([P, 2, P]),
                            bank[pair[odd]][:, 2 * half * P:2 * (half + 1) * P].rearrange("p (a b) -> p a b", a=2))
                        if half == 1 and odd == 1:
                            e.then_inc(lvl_done, 1)
                        else:
                            step(e)
                    if half == 1 and i < len(LEVELS):
                        v.wait_ge(lvl_done, i // 2 + 1)
                v.sem_clear(lvl_ready)
                v.wait_ge(num_ready, c + 1)
                den = [bank[3 + 2 * b][:, :].rearrange("p (a b) -> p a b", a=2)[:, :, M_DIM] for b in range(2)]
                for b in range(2):
                    step(nc.vector.scalar_tensor_tensor(r4[:, 2 * b:2 * b + 2], den[b], -1.0,
                                                        cols[:, M_HEADS + 2 * b:M_HEADS + 2 * b + 2], ALU.mult, ALU.max))
                settle()
                for b in range(2):
                    step(nc.vector.tensor_tensor(r4[:, 2 * b:2 * b + 2], den[b], r4[:, 2 * b:2 * b + 2], ALU.max))
                settle()
                link(nc.vector.reciprocal(ri4[:, :], r4[:, :]))
                for b in range(2):
                    e = nc.vector.tensor_tensor(
                        y[:, b * 256:(b + 1) * 256].rearrange("p (a b) -> p a b", a=2),
                        bank[3 + 2 * b][:, :].rearrange("p (a b) -> p a b", a=2)[:, :, 0:M_DIM],
                        ri4[:, 2 * b:2 * b + 2].unsqueeze(2).to_broadcast([P, 2, M_DIM]), ALU.mult)
                    if b == 0:
                        step(e)
                e.then_inc(h_ready, 1)
                v.wait_ge(cu_ready, c + 1)
                for h in range(M_HEADS):
                    src = bank[4 - 2 * (h // 2)][:, (h % 2) * 256:(h % 2) * 256 + M_DIM + 1]
                    e = nc.vector.scalar_tensor_tensor(c_st[:, h, :], c_st[:, h, :], dec[:, h:h + 1], src,
                                                       ALU.mult, ALU.add)
                    if h < M_HEADS - 1:
                        step(e)
                e.then_inc(c_done, 1)
                v.wait_ge(sqm_ready, c + 1)
                step(nc.vector.tensor_reduce(ss8[:, 0:M_HEADS], sq.rearrange("p (a b) -> p a b", a=4), axis=AX.X,
                                             op=ALU.add))
                v.wait_ge(sqg_ready, c + 1)
                link(nc.vector.tensor_reduce(ss8[:, M_HEADS:], em[:, :, :], axis=AX.X, op=ALU.add))
                nc.vector.tensor_scalar(ms8[:, :], ss8[:, :], 4.0 / M_DIM, 4.0 * EPS, ALU.mult, ALU.add).then_inc(ss_ready, 1)
                v.wait_ge(su_ready, c + 1)
                for h in range(G_HEADS):
                    part, j = slice(G_K * (h % 2), G_K * (h % 2) + G_K), h // 2
                    e = nc.vector.scalar_tensor_tensor(s_st[part, j, :], s_st[part, j, :], eb[part, j, P - 1:P],
                                                       bank[3][part, h * P:(h + 1) * P], ALU.mult, ALU.add)
                    if h < G_HEADS - 1:
                        step(e)
                e.then_inc(s_done, 1)
                v.wait_ge(rs_ready, c + 1)
                v.wait_ge(h_ready, c + 1)
                ym = y[:, 0:M_WIDTH].rearrange("p (a b) -> p a b", a=4)
                yg = y[:, M_WIDTH:].rearrange("p (a b) -> p a b", a=4)
                for odd in range(2):
                    e = nc.vector.tensor_tensor(yg[:, odd::2, :], bank[6 + odd][:, 0:2 * P].rearrange("p (a b) -> p a b", a=2),
                                                rs8[:, M_HEADS + odd::2].unsqueeze(2).to_broadcast([P, 2, P]), ALU.mult)
                    if odd == 0:
                        step(e)
                e.then_inc(og_used, 1)
                link(nc.vector.tensor_tensor(ym, ym, rs8[:, 0:M_HEADS].unsqueeze(2).to_broadcast([P, 4, P]), ALU.mult))
                step(nc.vector.scalar_tensor_tensor(y[:, 0:M_WIDTH], o_th[par][:, :], 1.0, y[:, 0:M_WIDTH],
                                                    ALU.add, ALU.mult))
                v.wait_ge(og_used, c + 1)
                nc.vector.tensor_tensor(y[:, M_WIDTH:], y[:, M_WIDTH:], gate2[par][:, :], ALU.mult).then_inc(y_ready, 1)
                if not last:
                    out_gate(c + 1, nxt)
                settle()
                v.sem_clear(dve_seq)
                n[0] = 0

            settle()
            v.sem_clear(dve_seq)
            n[0] = 0
            chunk_program(v, mix)



def router_phase(nc, t, c, h_all, logits):
    ctx = ExitStack()
    with ctx:
        def sb(name, shape, dt=F32):
            return ctx.enter_context(nc.sbuf_tensor(name, shape, dt))

        def sem(name):
            return ctx.enter_context(nc.semaphore(name))

        views = c["views"]
        yT, h, y_hi, y_lo = [[views[f"{n}{p}"] for p in range(2)] for n in ("yT_", "h_", "y_hi", "y_lo")]
        xn = [views[f"xn2_{p}"].rearrange("q (k p) -> q k p", k=KT) for p in range(2)]
        sq, zeros = views["squares"], views["zeros"]
        w_hi, w_lo = [views[n].rearrange("p (k n) -> p k n", k=KT) for n in ("w_hi", "w_lo")]
        wr = sb("wr", [P, KT, N_GROUPS + N_EXPERTS])
        br = sb("br", [P, N_GROUPS + N_EXPERTS])
        xT = sb("xn2T", [P, KT, P])
        g2 = sb("g2", [P, D_MODEL])
        ss, ms, rs = sb("ss2", [P, 1]), sb("ms2", [P, 1]), sb("rs2", [P, 1])
        bank = [ctx.enter_context(nc.psum_tensor(f"rbank{i}", [P, 512], F32)) for i in range(8)]

        y_loaded, x_loaded = c["y_loaded"], c["x_loaded"]
        r_loaded, g_loaded, zeroed, zeros_stored = sem("wr_loaded"), sem("g2_loaded"), sem("zeroed"), sem("zeros_stored")
        xn_free = [sem(f"xn2_free{p}") for p in range(2)]
        y_hi_out, y_lo_out = sem("y_hi_out"), sem("y_lo_out")
        o1_ready, o_ready, h1_ready, h_ready, h_kept = (sem("o1_ready"), sem("o2_ready"), sem("h1_ready"), sem("h2_ready"),
                                                        sem("h2_kept"))
        ss_ready, rs_ready, xn_ready = sem("ss2_ready"), sem("rs2_ready"), sem("xn2_ready")
        xT_ready, xT_out, lg_ready = sem("x2T_ready"), sem("x2T_out"), sem("lg_ready")
        lg_free = sem("lg_free")
        pool_seq = sem("pool_seq2")
        block = ctx.enter_context(nc.Block())

        def tiles(eng, body):
            with eng.Fori(0, TILES // 2 - 1) as j:
                for p in range(2):
                    body(j * 2 + p, j, p)
            for p in range(2):
                body(TILES - 2 + p, TILES // 2 - 1, p)

        def within(i, ahead):
            return not (isinstance(i, int) and i + ahead >= TILES)

        @block.sync
        def _(sp):
            sp.dma_start(g2[:, :], t["norm2_g"].partition_broadcast(P)).then_inc(g_loaded, 16)
            sp.dma_start(wr[:, :, 0:N_GROUPS], t["wr_g"].rearrange("(p k) n -> p k n", k=KT)).then_inc(r_loaded, 16)
            sp.dma_start(wr[:, :, N_GROUPS:], t["wr_e"].rearrange("(p k) n -> p k n", k=KT)).then_inc(r_loaded, 16)
            sp.dma_start(br[:, 0:N_GROUPS], t["br_g"].partition_broadcast(P)).then_inc(r_loaded, 16)
            sp.dma_start(br[:, N_GROUPS:], t["br_e"].partition_broadcast(P)).then_inc(r_loaded, 16)
            sp.dma_start(c["gf"][:, :], t["final_norm_g"].partition_broadcast(P)).then_inc(g_loaded, 16)
            sp.wait_ge(zeroed, 1)

            def body(i, j, p):
                if within(i, 2):
                    sp.wait_ge(y_lo_out, i + 1)
                    sp.dma_start(yT[p], at(t["yT"], i + 3)).then_inc(y_loaded[p], 16)
                sp.wait_ge(xn_ready, i + 1)
                sp.dma_start(at(t["xn2"], i), xn[p].rearrange("q k p -> q (k p)")).then_inc(xn_free[p], 16)
                if within(i, 2):
                    sp.wait_ge(h_kept, i + 1)
                    sp.dma_start(h[p], at(t["x"], i + 2)).then_inc(x_loaded[p], 16)
                for k in range(ZERO_BLOCKS // TILES):
                    sp.dma_start(at(t["y_slots"], i * (ZERO_BLOCKS // TILES) + (FULL_BLOCKS + k)),
                                 zeros).then_inc(zeros_stored, 16)

            tiles(sp, body)
            for p in range(2):
                sp.wait_ge(xn_free[p], 1 + 16 * TILES // 2)
            sp.wait_ge(g_loaded, 32)
            sp.wait_ge(zeros_stored, 16 * ZERO_BLOCKS)

        @block.gpsimd
        def _(pool):
            pool.memset(c["zero"][:, :], 0.0).then_inc(pool_seq, 1)
            for p in range(2):
                pool.sem_inc(xn_free[p], 1)
            pool.wait_ge(pool_seq, 1)
            pool.sem_clear(pool_seq)
            pool.memset(zeros, 0.0).then_inc(zeroed, 1)

            def body(i, j, p):
                pool.wait_ge(ss_ready, i + 1)
                pool.tensor_tensor(ms[:, :], ss[:, :], c["eps_col"][:, :], ALU.add).then_inc(pool_seq, 1)
                pool.wait_ge(pool_seq, 1)
                pool.sem_clear(pool_seq)
                pool.tensor_tensor(rs[:, :], ms[:, :], c["mhalf"][:, 0:1], ALU.pow).then_inc(rs_ready, 1)

            tiles(pool, body)

        @block.scalar
        def _(act):
            def high(i, j, p):
                act.wait_ge(y_loaded[p], (j + 1) * 16)
                wait(act, o_ready, i - 1)
                wait(act, y_lo_out, i - 1)
                nc.scalar.activation(y_hi[p], yT[p], ACT.Copy).then_inc(y_hi_out, 1)

            def square(i, j, p):
                act.wait_ge(h_ready, i + 1)
                wait(act, rs_ready, i)
                nc.scalar.activation(sq, h[p], ACT.Square, scale=D_MODEL ** -0.5, accum_out=ss[:, :]).then_inc(ss_ready, 1)

            def route(i, j, p):
                for half in range(2):
                    act.wait_ge(xT_ready, i * 2 + (half + 1))
                    nc.scalar.activation(xT[:, 4 * half:4 * half + 4, :],
                                         bank[4 + half][:, :].rearrange("p (a b) -> p a b", a=4), ACT.Copy).then_inc(xT_out, 1)

            high(0, 0, 0)
            high(1, 0, 1)
            square(0, 0, 0)

            def body(i, j, p):
                if within(i, 2):
                    high(i + 2, j + 1, p)
                route(i, j, p)
                if within(i, 1):
                    square(i + 1, j + p, 1 - p)

            tiles(act, body)

        @block.tensor
        def _(pe):
            pe.wait_ge(r_loaded, 64)
            pe.sem_inc(lg_free, 1)

            def project(i, j, p, half):
                for k in range(KT):
                    cols = slice(half * 512, half * 512 + 512)
                    hi, lo = y_hi[p][:, k * P:(k + 1) * P], y_lo[p][:, k * P:(k + 1) * P]
                    dst = bank[2 * p + half][:, :]
                    nc.tensor.matmul(dst, hi, w_hi[:, k, cols], start=(k == 0), stop=False)
                    nc.tensor.matmul(dst, hi, w_lo[:, k, cols], start=False, stop=False)
                    mm = nc.tensor.matmul(dst, lo, w_hi[:, k, cols], start=False, stop=(k == KT - 1))
                return mm

            def project1(i, j, p):
                pe.wait_ge(y_lo_out, i + 1)
                wait(pe, h_ready, i - 1)
                project(i, j, p, 0).then_inc(o1_ready, 1)

            def project2(i, j, p):
                project(i, j, p, 1).then_inc(o_ready, 1)

            project1(0, 0, 0)
            project2(0, 0, 0)

            def body(i, j, p):
                if within(i, 1):
                    project1(i + 1, j + p, 1 - p)
                pe.wait_ge(xn_ready, i + 1)
                for k in range(KT):
                    mm = nc.tensor.transpose(bank[4 + k // 4][:, (k % 4) * P:(k % 4 + 1) * P], xn[p][:, k, :],
                                             c["ident"][:, :])
                    if k % 4 == 3:
                        mm.then_inc(xT_ready, 1)
                if within(i, 1):
                    project2(i + 1, j + p, 1 - p)
                pe.wait_ge(xT_out, i * 2 + 2)
                pe.wait_ge(lg_free, i + 1)
                for k in range(KT):
                    mm = nc.tensor.matmul(bank[6][:, 0:N_GROUPS + N_EXPERTS], xT[:, k, :], wr[:, k, :],
                                          start=(k == 0), stop=(k == KT - 1))
                mm.then_inc(lg_ready, 1)

            tiles(pe, body)

        @block.vector
        def _(v):
            def low(i, j, p):
                v.wait_ge(y_hi_out, i + 1)
                nc.vector.tensor_tensor(y_lo[p], yT[p], y_hi[p].bitcast(F32), ALU.subtract).then_inc(y_lo_out, 1)

            def residual(i, j, p):
                v.wait_ge(x_loaded[p], (j + 1) * 16)
                v.wait_ge(o1_ready, i + 1)
                nc.vector.tensor_tensor(h[p][:, 0:512], h[p][:, 0:512], bank[2 * p][:, :], ALU.add).then_inc(h1_ready, 1)
                v.wait_ge(o_ready, i + 1)
                nc.vector.tensor_tensor(h[p][:, 512:], h[p][:, 512:], bank[2 * p + 1][:, :], ALU.add).then_inc(h_ready, 1)

            def normed(i, j, p):
                v.wait_ge(rs_ready, i + 1)
                v.wait_ge(h1_ready, i + 1)
                v.wait_ge(h_ready, i + 1)
                v.wait_ge(xn_free[p], j * 16 + 1)
                nc.vector.scalar_tensor_tensor(xn[p], h[p].rearrange("t (p k) -> t k p", k=KT), rs[:, :],
                                               g2[:, :].rearrange("t (p k) -> t k p", k=KT),
                                               ALU.mult, ALU.mult).then_inc(xn_ready, 1)

            def kept(i, j, p):
                dst = h_all[:, i, :] if isinstance(i, int) else h_all[:, bass.ds(i, 1), :].rearrange("p o c -> p (o c)")
                nc.vector.tensor_tensor(dst, h[p], c["zero"][:, 0:1].to_broadcast([P, D_MODEL]), ALU.add).then_inc(h_kept, 1)

            low(0, 0, 0)
            low(1, 0, 1)
            v.wait_ge(g_loaded, 32)
            residual(0, 0, 0)
            normed(0, 0, 0)
            kept(0, 0, 0)

            def body(i, j, p):
                if within(i, 2):
                    low(i + 2, j + 1, p)
                if within(i, 1):
                    residual(i + 1, j + p, 1 - p)
                    normed(i + 1, j + p, 1 - p)
                v.wait_ge(lg_ready, i + 1)
                dst = logits[:, i, :] if isinstance(i, int) else logits[:, bass.ds(i, 1), :].rearrange("p o c -> p (o c)")
                nc.vector.tensor_tensor(dst, bank[6][:, 0:N_GROUPS + N_EXPERTS], br[:, :], ALU.add).then_inc(lg_free, 1)
                if within(i, 1):
                    kept(i + 1, j + p, 1 - p)

            tiles(v, body)
            v.wait_ge(lg_free, TILES + 1)


def experts_phase(nc, t, c, h_all, logits):
    ctx = ExitStack()
    with ctx:
        def sb(name, shape, dt=F32):
            return ctx.enter_context(nc.sbuf_tensor(name, shape, dt))

        def sem(name):
            return ctx.enter_context(nc.semaphore(name))

        E, G, NT = N_EXPERTS, N_GROUPS, TILES
        w_size = KT * D_EXPERT
        region = c["region"]
        w_all = region[:, 0:SLOTS * 3 * w_size].rearrange("p (m f) -> p m f", f=D_EXPERT)
        w_slot = w_all[:, :, :].rearrange("p (s m) f -> p s (m f)", s=SLOTS)
        rest = region[:, SLOTS * 3 * w_size:SLOTS * 3 * w_size + 4 * D_MODEL].rearrange("p (b d) -> p b d", d=D_MODEL)
        xg_all, xT_all, y_all = rest[:, 0:2, :], rest[:, 2:4, :], sb("yb", [P, 2, D_MODEL])
        xg = [xg_all[:, p, :].rearrange("q (a b) -> q a b", a=KT) for p in range(2)]
        xT = [xT_all[:, p, :].rearrange("q (a b) -> q a b", a=KT) for p in range(2)]
        sg = sb("silu_gate", [P, D_EXPERT])
        hid = [sb(f"hid{p}", [P, 2, P]) for p in range(2)]
        hidT = sb("hidT", [P, 2, P])
        yb = [y_all[:, p, :] for p in range(2)]
        iota_e = sb("iota_e", [P, E])
        iota_g = sb("iota_g", [P, G])
        iota_i = sb("iota_i", [P, E], I32)
        tok = sb("tok", [P, NT])
        tok_i = sb("tok_i", [P, NT], I32)
        tri = sb("tri", [P, P])
        ones = sb("ones", [P, P])
        work = y_all[:, :, :].rearrange("p a (b i e) -> p (a b) i e", b=2, e=E)
        oh = [work[:, i] for i in range(2)]
        lm, tmp = work[:, 2], work[:, 3]
        slotv = sb("slotv", [P, NT, E])
        ohg = sb("ohg", [P, NT, G])
        gt = sb("group_work", [P, NT, G])[:, :, :]
        mx = [sb(f"mx{i}", [P, NT]) for i in range(3)]
        idx1 = sb("idx1", [P, NT])
        wt = [sb(f"wt{i}", [P, NT]) for i in range(2)]
        ex = sb("ex", [P, NT])
        slot_f = [sb(f"slot_f{i}", [P, NT]) for i in range(2)]
        slot_i = [sb(f"slot_i{i}", [P, NT], I32) for i in range(2)]
        cnt = sb("cnt", [P, E])
        cnt_i = sb("cnt_i", [P, E], I32)
        pad_end = sb("pad_end", [P, E])
        start = sb("start", [P, E])
        NB = BLOCKS - 2
        blk_i = xg_all[0:1, :, :].rearrange("p a (b e) -> p (a b) e", e=E).bitcast(I32)
        blk = xT_all[0:1, :, :].rearrange("p a (b e) -> p (a b) e", e=E)
        exp_f = sb("exp_f", [1, NB])
        exp_i = sb("exp_i", [1, BLOCKS], I32)
        free_i = sb("free_i", [1, E], I32)
        nblk_i = sb("nblk_i", [1, 1], I32)
        zrow = sb("zrow", [BLOCKS, P])
        srow = sb("srow", [BLOCKS, P])
        sidT = sb("sidT", [P, BLOCKS])
        cur = [sb(f"cur{p}", [P, 1], I32) for p in range(2)]
        cur2 = [sb(f"cur2{p}", [P, 1], I32) for p in range(2)]
        zero_i = sb("zero_i", [P, 1], I32)
        zero_f = sb("zero_f", [P, 1])
        fsq = xg_all[:, 0, :]
        fss, fms, frs = sb("fss", [P, 1]), sb("fms", [P, 1]), sb("frs", [P, 2])
        bank = [ctx.enter_context(nc.psum_tensor(f"ebank{i}", [P, 512], F32)) for i in range(8)]

        w_loaded = [sem(f"expert_loaded{i}") for i in range(SLOTS)]
        consts, zeros_out, scattered, srow_loaded, sidT_ready = (sem("consts3"), sem("zeros_out"), sem("scattered"),
                                                                 sem("srow_loaded"), sem("sidT_ready"))
        tables, slots_ready, oh_ready, rank_ready, exm, exm_done = (sem("tables"), sem("slots_ready"), sem("oh_ready"),
                                                                    sem("rank_ready"), sem("exm"), sem("exm_done"))
        sid_out = sem("sid_out")
        cur_ready = sem("cur_ready")
        xg_loaded = [sem(f"xg_loaded{p}") for p in range(2)]
        xt_ready, xT_out, gu_ready, sg_ready, h_ready = (sem("xt_ready"), sem("xT_out3"), sem("gu_ready"),
                                                         sem("sg_ready"), sem("h_ready3"))
        ht_ready, hT_out, d_ready, ya_out, yb_out = sem("ht_ready"), sem("hT_out"), sem("d_ready"), sem("ya_out"), sem("yb_out")
        yb_free = [sem(f"yb_free{p}") for p in range(2)]
        got = [sem(f"got{r}") for r in range(RING)]
        sum_ready, fss_ready, frs_ready, o_ready = sem("sum_ready"), sem("fss_ready"), sem("frs_ready"), sem("o_ready3")
        o_stored = [sem(f"o_stored{r}") for r in range(RING)]
        dve_seq, pool_seq = sem("dve_seq3"), sem("pool_seq3")
        block = ctx.enter_context(nc.Block())

        def blocks(eng, body):
            n = eng.value_load(nblk_i[0:1, 0:1], min_val=SEQ * TOP_K // P, max_val=BLOCKS - 3)
            with eng.Fori(0, (BLOCKS - 2) // 2) as j:
                for q in range(2):
                    b = j * 2 + (1 + q)
                    with eng.If(b < n + 1):
                        body(b, j, 1 - q)
            return n

        @block.sync
        def _(sp):
            def load(e, s):
                def src(name, k):
                    w = t[name][e:e + 1] if isinstance(e, int) else t[name][bass.ds(e, 1)]
                    return w.rearrange("o (p k) f -> (o p) (k f)", k=k)
                for i, (name, k) in enumerate((("w_gate", KT), ("w_up", KT), ("w_down", D_EXPERT // P))):
                    sp.dma_start(w_slot[:, s, i * w_size:(i + 1) * w_size], src(name, k)).then_inc(w_loaded[s], 16)

            for s in range(SLOTS):
                sp.sem_inc(w_loaded[s], 1)
            for p in range(2):
                sp.sem_inc(yb_free[p], 1)
            sp.wait_ge(consts, 1)
            sp.dma_start(t["slot_tok"].rearrange("(b p) o -> b (p o)", p=P), zrow[:, :]).then_inc(zeros_out, 16)
            for s in range(SLOTS):
                load(s, s)
            sp.wait_ge(scattered, 16 * 2 * NT)
            sp.dma_start(srow[:, :], t["slot_tok"].rearrange("(b p) o -> b (p o)", p=P)).then_inc(srow_loaded, 16)
            sp.wait_ge(tables, 1)
            with sp.Fori(1, E // SLOTS) as j:
                for s in range(SLOTS):
                    e = j * SLOTS + s
                    done = sp.value_load(free_i[0:1, bass.ds(e, 1)], min_val=0, max_val=BLOCKS)
                    sp.wait_ge(d_ready, done + 1)
                    load(e, s)
            for i in range(NT):
                sp.wait_ge(o_ready, i + 1)
                sp.dma_start(t["out"][i], w_slot[:, i % RING, 0:D_MODEL]).then_inc(o_stored[i % RING], 16)
            for r in range(RING):
                sp.wait_ge(o_stored[r], 16 * (NT // RING))

        @block.gpsimd
        def _(pool):
            n = [0]

            def link(ins):
                n[0] += 1
                ins.then_inc(pool_seq, 1)
                pool.wait_ge(pool_seq, n[0])

            link(pool.memset(zrow[:, :], 0.0))
            link(pool.memset(zero_i[:, :], 0))
            link(pool.memset(zero_f[:, :], 0.0))
            link(pool.memset(ones[:, :], 1.0))
            link(pool.memset(tri[:, :], 1.0))
            link(pool.affine_select(out=tri[:, :], in_=tri[:, :], compare_op=ALU.is_ge, fill=0.0, base=-1,
                                    pattern=[[1, P]], channel_multiplier=-1))
            link(pool.iota(iota_i[:, :], pattern=[[1, E]], base=-E, channel_multiplier=0))
            link(pool.tensor_copy(iota_e[:, :], iota_i[:, :]))
            link(pool.iota(iota_i[:, 0:G], pattern=[[1, G]], base=-G, channel_multiplier=0))
            link(pool.tensor_copy(iota_g[:, :], iota_i[:, 0:G]))
            link(pool.iota(tok_i[:, :], pattern=[[P, NT]], base=0, channel_multiplier=1))
            link(pool.tensor_copy(tok[:, :], tok_i[:, :]))
            link(pool.iota(blk_i, pattern=[[1, NB], [0, E]], base=0, channel_multiplier=0))
            pool.tensor_copy(blk, blk_i).then_inc(consts, 1)
            pool.wait_ge(consts, 1)
            pool.wait_ge(zeros_out, 16)
            pool.wait_ge(slots_ready, 1)
            for i in range(NT):
                for k in range(TOP_K):
                    pool.indirect_dma_start(t["slot_tok"], bass.IndirectOffsetOnAxis(ap=slot_i[k][:, i:i + 1], axis=0),
                                            tok[:, i:i + 1], None).then_inc(scattered, 16)
            rows = t["xn2"].rearrange("i p c -> (i p) c")

            def gather(b, q):
                pool.wait_ge(cur_ready, b + 1)
                pool.tensor_tensor(cur2[q][:, :], cur[q][:, :], zero_i[:, :], ALU.add).then_inc(pool_seq, 1)
                pool.wait_ge(pool_seq, 1)
                pool.sem_clear(pool_seq)
                pool.indirect_dma_start(xg_all[:, q, :], None, rows,
                                        bass.IndirectOffsetOnAxis(ap=cur2[q][:, 0:1], axis=0)).then_inc(xg_loaded[q], 16)

            pool.sem_clear(pool_seq)
            gather(0, 0)
            gather(1, 1)

            def body(b, j, p):
                pool.wait_ge(xt_ready, b)
                gather(b + 1, 1 - p)

            nb = blocks(pool, body)
            y_rows = t["y_slots"].rearrange("b p c -> (b p) c")
            pool.wait_ge(d_ready, nb + 1)
            for p in range(2):
                pool.wait_ge(yb_free[p], ((nb + (1 - p)) >> 1) * 16 + 1)
            pool.tensor_tensor(cur2[0][:, :], cur[0][:, :], zero_i[:, :], ALU.add).then_inc(pool_seq, 1)
            pool.wait_ge(pool_seq, 1)
            pool.sem_clear(pool_seq)

            def collect(i):
                r = i % RING
                if i >= RING:
                    pool.wait_ge(o_stored[r], 16 * (i // RING))
                for k in range(TOP_K):
                    pool.indirect_dma_start(w_slot[:, r, k * D_MODEL:(k + 1) * D_MODEL], None, y_rows,
                                            bass.IndirectOffsetOnAxis(ap=slot_i[k][:, i:i + 1], axis=0)).then_inc(got[r], 16)

            for i in range(RING - 1):
                collect(i)
            for i in range(NT):
                if i + RING - 1 < NT:
                    collect(i + RING - 1)
                pool.wait_ge(fss_ready, i + 1)
                pool.tensor_tensor(fms[:, :], fss[:, :], c["eps_col"][:, :], ALU.add).then_inc(pool_seq, 1)
                pool.wait_ge(pool_seq, i + 1)
                wait(pool, o_ready, i - 1)
                pool.tensor_tensor(frs[:, i % 2:i % 2 + 1], fms[:, :], c["mhalf"][:, 0:1], ALU.pow).then_inc(frs_ready, 1)

        @block.scalar
        def _(act):
            act.wait_ge(exm, 1)
            nc.scalar.activation(gt, gt, ACT.Exp).then_inc(exm_done, 1)
            act.wait_ge(exm, 2)
            nc.scalar.activation(ex[:, :], ex[:, :], ACT.Exp).then_inc(exm_done, 1)
            act.wait_ge(tables, 1)

            def silu(b, p):
                act.wait_ge(gu_ready, b + 1)
                wait(act, h_ready, b)
                nc.scalar.activation(sg[:, :], bank[2 + p][:, 0:D_EXPERT], ACT.Silu).then_inc(sg_ready, 1)

            silu(0, 0)

            def body(b, j, p):
                silu(b, p)
                act.wait_ge(ht_ready, b)
                nc.scalar.activation(hidT[:, :, :], bank[4][:, 0:2 * P].rearrange("p (a b) -> p a b", a=2),
                                     ACT.Copy).then_inc(hT_out, 1)
                act.wait_ge(d_ready, b + 1)
                act.wait_ge(yb_free[1 - p], j * 16 + 1)
                nc.scalar.activation(yb[1 - p][:, 0:512], bank[5][:, :], ACT.Copy).then_inc(ya_out, 1)
                act.wait_ge(yb_out, b)
                act.wait_ge(ya_out, b)
                act.dma_start(at(t["y_slots"], b - 1), yb[1 - p][:, :]).then_inc(yb_free[1 - p], 16)

            blocks(act, body)
            for i in range(NT):
                act.wait_ge(sum_ready, i + 1)
                wait(act, frs_ready, i)
                nc.scalar.activation(fsq, w_slot[:, i % RING, 0:D_MODEL], ACT.Square, scale=D_MODEL ** -0.5,
                                     accum_out=fss[:, :]).then_inc(fss_ready, 1)

        @block.tensor
        def _(pe):
            pe.sem_inc(d_ready, 1)
            pe.wait_ge(consts, 1)
            pe.wait_ge(oh_ready, 1)
            flat = lm.rearrange("p a b -> p (a b)")
            nc.tensor.matmul(bank[0][:, :], tri[:, :], flat, start=True, stop=True)
            nc.tensor.matmul(bank[1][:, :], ones[:, :], flat, start=True, stop=True).then_inc(rank_ready, 1)
            pe.wait_ge(srow_loaded, 16)
            pe.wait_ge(tables, 1)
            nc.tensor.transpose(bank[7][:, 0:BLOCKS], srow[:, :], c["ident"][0:BLOCKS, 0:BLOCKS]).then_inc(sidT_ready, 1)
            pe.wait_ge(sid_out, 1)

            def transpose_x(b, q, count):
                pe.wait_ge(xg_loaded[q], count)
                wait(pe, xT_out, b)
                for k in range(KT):
                    mm = nc.tensor.transpose(bank[k // 4][:, (k % 4) * P:(k % 4 + 1) * P], xg[q][:, k, :], c["ident"][:, :])
                mm.then_inc(xt_ready, 1)

            def gate_up(b, p):
                e = pe.value_load(exp_i[0:1, b:b + 1] if isinstance(b, int) else exp_i[0:1, bass.ds(b, 1)],
                                  min_val=0, max_val=E - 1)
                pe.wait_ge(xT_out, b + 1)
                for s in range(SLOTS):
                    pe.wait_ge(w_loaded[s], ((e + (SLOTS - s)) // SLOTS) * 48 + 1)
                slot = e % SLOTS
                for i in range(2):
                    for k in range(KT):
                        w = w_all[:, bass.ds(slot * (3 * KT) + (i * KT + k), 1), :].rearrange("p o f -> p (o f)")
                        mm = nc.tensor.matmul(bank[2 + p][:, i * D_EXPERT:(i + 1) * D_EXPERT], xT[p][:, k, :], w,
                                              start=(k == 0), stop=(k == KT - 1))
                mm.then_inc(gu_ready, 1)

            transpose_x(0, 0, 16)
            gate_up(0, 0)
            transpose_x(1, 1, 16)

            def body(b, j, p):
                gate_up(b, p)
                pe.wait_ge(h_ready, b)
                for i in range(2):
                    mm = nc.tensor.transpose(bank[4][:, i * P:(i + 1) * P], hid[1 - p][:, i, :], c["ident"][:, :])
                mm.then_inc(ht_ready, 1)
                transpose_x(b + 1, 1 - p, (j + 2) * 16)
                e = pe.value_load(exp_i[0:1, bass.ds(b - 1, 1)], min_val=0, max_val=E - 1)
                slot = e % SLOTS
                pe.wait_ge(hT_out, b)
                for half in range(2):
                    for i in range(2):
                        w = w_all[:, bass.ds(slot * (3 * KT) + (2 * KT + (i * D_MODEL + half * 512) // D_EXPERT), 2), :]
                        mm = nc.tensor.matmul(bank[5 + half][:, :], hidT[:, i, :], w.rearrange("p o f -> p (o f)"),
                                              start=(i == 0), stop=(i == 1))
                mm.then_inc(d_ready, 1)

            blocks(pe, body)

        @block.vector
        def _(v):
            n = [0]

            def step(ins):
                n[0] += 1
                ins.then_inc(dve_seq, 1)

            def settle():
                v.wait_ge(dve_seq, n[0])

            def link(ins):
                step(ins)
                settle()

            TT, TS, STT, RED = (nc.vector.tensor_tensor, nc.vector.tensor_scalar, nc.vector.scalar_tensor_tensor,
                                nc.vector.tensor_reduce)
            v.wait_ge(consts, 1)
            lg, le = logits[:, :, 0:G], logits[:, :, G:]

            def first_max(one_hot, values, m, work, iota, width):
                shape = [P, NT, width]
                link(RED(m[:, :], values, axis=AX.X, op=ALU.max))
                link(TT(work, values, m[:, :].unsqueeze(2).to_broadcast(shape), ALU.is_equal))
                link(TT(work, work, iota[:, :].unsqueeze(1).to_broadcast(shape), ALU.mult))
                link(RED(idx1[:, :], work, axis=AX.X, op=ALU.min))
                link(TT(one_hot, iota[:, :].unsqueeze(1).to_broadcast(shape), idx1[:, :].unsqueeze(2).to_broadcast(shape),
                        ALU.is_equal))

            first_max(ohg[:, :, :], lg, mx[0], gt, iota_g, G)
            TT(gt, lg, mx[0][:, :].unsqueeze(2).to_broadcast([P, NT, G]), ALU.subtract).then_inc(exm, 1)
            link(TS(ohg[:, :, :], ohg[:, :, :], -1.0, -NEG, ALU.add, ALU.mult))
            link(TT(lm.rearrange("p i (g e) -> p i g e", g=G), le.rearrange("p i (g e) -> p i g e", g=G),
                    ohg[:, :, :].unsqueeze(3).to_broadcast([P, NT, G, PER_GROUP]), ALU.add))
            first_max(oh[0], lm, mx[1], tmp, iota_e, E)
            link(STT(lm, oh[0], 3 * NEG, lm, ALU.mult, ALU.add))
            first_max(oh[1], lm, mx[2], tmp, iota_e, E)
            TT(lm, oh[0], oh[1], ALU.add).then_inc(oh_ready, 1)
            v.wait_ge(exm_done, 1)
            TT(ex[:, :], mx[2][:, :], mx[1][:, :], ALU.subtract).then_inc(exm, 1)
            link(RED(mx[0][:, :], gt, axis=AX.X, op=ALU.add))
            v.wait_ge(exm_done, 2)
            link(STT(wt[0][:, :], ex[:, :], 1.0, mx[0][:, :], ALU.add, ALU.mult))
            link(nc.vector.reciprocal(wt[0][:, :], wt[0][:, :]))
            link(TT(wt[1][:, :], wt[0][:, :], ex[:, :], ALU.mult))
            v.wait_ge(rank_ready, 1)
            tot = bank[1][:, :].rearrange("p (i e) -> p i e", i=NT)
            link(RED(cnt[:, :], bank[1][:, :].rearrange("p (i e) -> p e i", i=NT), axis=AX.X, op=ALU.add))
            link(TS(cnt_i[:, :], cnt[:, :], float(P - 1), None, ALU.add))
            link(TS(cnt_i[:, :], cnt_i[:, :], P.bit_length() - 1, None, ALU.arith_shift_right))
            link(nc.vector.tensor_copy(cnt[:, :], cnt_i[:, :]))
            link(nc.vector.tensor_tensor_scan(pad_end[:, :], ones[:, 0:E], cnt[:, :], 0.0, ALU.mult, ALU.add))
            link(TT(start[:, :], pad_end[:, :], cnt[:, :], ALU.subtract))
            link(TS(slotv[:, 0, :], start[:, :], float(P), None, ALU.mult))
            for i in range(NT - 1):
                link(TT(slotv[:, i + 1, :], slotv[:, i, :], tot[:, i, :], ALU.add))
            link(TT(slotv[:, :, :], slotv[:, :, :], bank[0][:, :].rearrange("p (i e) -> p i e", i=NT), ALU.add))
            for k in range(TOP_K):
                link(TT(tmp, oh[k], slotv[:, :, :], ALU.mult))
                link(RED(slot_f[k][:, :], tmp, axis=AX.X, op=ALU.add))
            link(nc.vector.tensor_copy(slot_i[0][:, :], slot_f[0][:, :]))
            nc.vector.tensor_copy(slot_i[1][:, :], slot_f[1][:, :]).then_inc(slots_ready, 1)
            link(TT(blk, blk, pad_end[0:1, :].unsqueeze(1).to_broadcast([1, NB, E]), ALU.is_ge))
            link(RED(exp_f[:, :], blk, axis=AX.X, op=ALU.add))
            link(nc.vector.memset(exp_i[:, NB:], 0))
            link(TS(exp_i[:, 0:NB], exp_f[:, :], float(E - 1), None, ALU.min))
            link(nc.vector.memset(free_i[:, 0:SLOTS], 0))
            link(nc.vector.tensor_copy(free_i[:, SLOTS:], pad_end[0:1, 0:E - SLOTS]))
            nc.vector.tensor_copy(nblk_i[:, :], pad_end[0:1, E - 1:E]).then_inc(tables, 1)
            v.wait_ge(tables, 1)
            v.wait_ge(sidT_ready, 1)
            nc.vector.tensor_copy(sidT[:, :], bank[7][:, 0:BLOCKS]).then_inc(sid_out, 1)
            v.wait_ge(sid_out, 1)
            v.sem_clear(dve_seq)
            n[0] = 0

            def index(b, q):
                src = sidT[:, b:b + 1] if isinstance(b, int) else sidT[:, bass.ds(b, 1)]
                TT(cur[q][:, :], src, zero_f[:, :], ALU.add).then_inc(cur_ready, 1)

            def out_x(b, q):
                v.wait_ge(xt_ready, b + 1)
                wait(v, gu_ready, b - 1)
                for half in range(2):
                    e = nc.vector.tensor_copy(xT[q][:, 4 * half:4 * half + 4, :],
                                              bank[half][:, :].rearrange("p (a b) -> p a b", a=4))
                    if half == 0:
                        e.then_inc(dve_seq, 1)
                e.then_inc(xT_out, 1)

            def hidden(b, p):
                v.wait_ge(sg_ready, b + 1)
                TT(hid[p][:, :, :], sg[:, :].rearrange("t (q j) -> t j q", j=2),
                   bank[2 + p][:, D_EXPERT:].rearrange("t (q j) -> t j q", j=2), ALU.mult).then_inc(h_ready, 1)

            index(0, 0)
            index(1, 1)
            out_x(0, 0)
            hidden(0, 0)
            out_x(1, 1)
            v.wait_ge(dve_seq, 2)
            v.sem_clear(dve_seq)

            def body(b, j, p):
                v.wait_ge(xg_loaded[1 - p], (j + 1) * 16)
                index(b + 1, 1 - p)
                hidden(b, p)
                out_x(b + 1, 1 - p)
                v.wait_ge(d_ready, b + 1)
                v.wait_ge(yb_free[1 - p], j * 16 + 1)
                nc.vector.tensor_copy(yb[1 - p][:, 512:], bank[6][:, :]).then_inc(yb_out, 1)
                v.wait_ge(dve_seq, 1)
                v.sem_clear(dve_seq)

            blocks(v, body)
            for i in range(NT):
                r = i % RING
                a, b = w_slot[:, r, 0:D_MODEL], w_slot[:, r, D_MODEL:2 * D_MODEL]
                v.wait_ge(got[r], 32 * (i // RING + 1))
                link(STT(a, a, wt[0][:, i:i + 1], h_all[:, i, :], ALU.mult, ALU.add))
                STT(a, b, wt[1][:, i:i + 1], a, ALU.mult, ALU.add).then_inc(sum_ready, 1)
                if i:
                    finish(nc, v, c, w_slot, frs, frs_ready, o_ready, sum_ready, i - 1)
            finish(nc, v, c, w_slot, frs, frs_ready, o_ready, sum_ready, NT - 1)


def finish(nc, v, c, w_slot, frs, frs_ready, o_ready, sum_ready, i):
    a = w_slot[:, i % RING, 0:D_MODEL]
    v.wait_ge(frs_ready, i + 1)
    v.wait_ge(sum_ready, i + 1)
    nc.vector.scalar_tensor_tensor(a, a, frs[:, i % 2:i % 2 + 1], c["gf"][:, :], ALU.mult, ALU.mult).then_inc(o_ready, 1)


def build(nc, t):
    t = dict(t)
    t["yT"] = nc.dram_tensor("yT_dram", (CHUNKS, P, D_MODEL), F32).ap()
    t["xn2"] = nc.dram_tensor("xn2_dram", (TILES, P, D_MODEL), F32).ap()
    t["slot_tok"] = nc.dram_tensor("slot_tok", (BLOCKS * P, 1), F32).ap()
    t["y_slots"] = nc.dram_tensor("y_slots", (BLOCKS - 2, P, D_MODEL), F32).ap()
    ctx = ExitStack()
    with ctx:
        def sb(name, shape, dt=F32):
            return ctx.enter_context(nc.sbuf_tensor(name, shape, dt))

        c = {"vec": sb("vec", [P, R_ALL]), "ident": sb("ident", [P, P]), "mhalf": sb("mhalf", [P, M_HEADS + G_HEADS]),
             "eps_col": sb("eps_col", [P, 1])}
        start = -(-nc.sbuf_base // 32) * 32
        c.update({"region": sb("region", [P, KT * IN_WIDTH]), "views": router_views(nc, start)})
        assert nc.sbuf_base >= start + 4 * KT * IN_WIDTH
        for name in ("y_loaded", "x_loaded"):
            c[name] = [ctx.enter_context(nc.semaphore(f"{name}_router{p}")) for p in range(2)]
        mixer_phase(nc, t, c)
        h_all = sb("h_all", [P, TILES, D_MODEL])
        logits = sb("logits", [P, TILES, N_GROUPS + N_EXPERTS])
        c["gf"], c["zero"] = sb("gf", [P, D_MODEL]), sb("zero", [P, 1])
        router_phase(nc, t, c, h_all, logits)
        experts_phase(nc, t, c, h_all, logits)


_WEIGHTS = ["norm1_g", "w_in", "conv_w", "conv_b", "gate_b", "m_norm_g", "a_w2", "a_b", "g_norm_g", "w_out", "norm2_g",
            "wr_g", "br_g", "wr_e", "br_e", "w_gate", "w_up", "w_down"]
_ROWS = {"norm1_g", "conv_b", "m_norm_g", "a_b", "g_norm_g", "norm2_g", "br_g", "br_e"}


def kernel(**inputs):
    import concourse.bacc as bacc
    import numpy as np
    from concourse.bass_utils import run_bass_kernel_spmd

    arrays = {"x": np.asarray(inputs["x"]).reshape(TILES, P, D_MODEL), "meta_tokens": np.asarray(inputs["meta_tokens"]),
              "final_norm_g": np.asarray(inputs["final_norm_g"])}
    for name in _WEIGHTS:
        a = np.asarray(inputs[name])
        arrays[name] = a if name in _ROWS else a[0]
    nc = bacc.Bacc("TRN2", target_bir_lowering=False, num_devices=1)
    t = {}
    for name, a in arrays.items():
        arrays[name] = np.ascontiguousarray(a)
        t[name] = nc.dram_tensor(name, a.shape, F32, kind="ExternalInput").ap()
    t["out"] = nc.dram_tensor("out", (TILES, P, D_MODEL), F32, kind="ExternalOutput").ap()
    build(nc, t)
    r = run_bass_kernel_spmd(nc, [arrays], core_ids=[0])
    return r.results[0]["out"].reshape(1, SEQ, D_MODEL)
```
